# Optimizing a Trainium2 kernel written in Bass

```python
import jax, jax.numpy as jnp
from jax import lax
import numpy as np

D_MODEL = 1024
BATCH = 1
SEQ = 512
DEPTH = 1

D_MIX = D_MODEL
D_A = D_MIX // 2
D_B = D_MIX - D_A
N_HEADS_A = 8
HEAD_DIM_A = D_A // N_HEADS_A
N_GROUPS_B = 8
GROUP_DIM_B = D_B // N_GROUPS_B
CHUNK = 128
CONV_WIDTH = 31
D_IN = 2 * D_A + 2 * D_B
D_FF = -(-8 * D_MODEL // (3 * 256)) * 256
N_MOD = 6
EPS = 1e-6


def rmsnorm(x, g):
    xf = x.astype(jnp.float32)
    y = xf * lax.rsqrt(jnp.mean(xf * xf, axis=-1, keepdims=True) + EPS)
    return (y * g.astype(jnp.float32)).astype(x.dtype)

def layernorm(x, g, b):
    xf = x.astype(jnp.float32)
    mu = jnp.mean(xf, axis=-1, keepdims=True)
    xc = xf - mu
    var = jnp.mean(xc * xc, axis=-1, keepdims=True)
    y = xc * lax.rsqrt(var + EPS) * g.astype(jnp.float32) + b.astype(jnp.float32)
    return y.astype(x.dtype)

def modulate(h, shift, scale):
    return h * (1 + scale[:, None, :]) + shift[:, None, :]

def spatial_gating_mixer(u, v, ln_g, ln_b, w_s, b_s):
    B, S, _ = v.shape
    v = layernorm(v, ln_g, ln_b)
    v = v.reshape(B, S // CHUNK, CHUNK, N_HEADS_A, HEAD_DIM_A)
    causal = jnp.tril(jnp.ones((CHUNK, CHUNK), dtype=bool))
    w = jnp.where(causal[None], w_s, jnp.zeros_like(w_s)).astype(v.dtype)
    mixed = jnp.einsum('hts,bcshd->bcthd', w, v) + b_s.T.astype(v.dtype)[None, None, :, :, None]
    return u * mixed.reshape(B, S, D_A)

def conformer_conv_mixer(val, gate, conv_w, conv_b, gn_g, gn_b):
    B, S, _ = val.shape
    y = val * jax.nn.sigmoid(gate)
    y = lax.conv_general_dilated(
        y, conv_w[:, None, :].astype(y.dtype), window_strides=(1,),
        padding=[(CONV_WIDTH - 1, 0)],
        dimension_numbers=('NWC', 'WIO', 'NWC'),
        feature_group_count=D_B) + conv_b.astype(y.dtype)
    y = y.reshape(B, S, N_GROUPS_B, GROUP_DIM_B)
    y = layernorm(y, gn_g.reshape(N_GROUPS_B, GROUP_DIM_B), gn_b.reshape(N_GROUPS_B, GROUP_DIM_B))
    return jax.nn.silu(y.reshape(B, S, D_B))

def first_inputs(seed: int = 0) -> dict:
    key = jax.random.key(seed)
    ks = jax.random.split(key, 24)
    f32 = jnp.float32
    nrm = lambda k, shape, s: jax.random.normal(k, shape, f32) * s
    L = DEPTH
    return {
        "x": jax.random.normal(ks[0], (BATCH, SEQ, D_MODEL), f32),
        "c": jax.random.normal(ks[1], (BATCH, D_MODEL), f32),
        "ada_w": nrm(ks[2], (L, D_MODEL, N_MOD * D_MODEL), D_MODEL ** -0.5),
        "ada_b": nrm(ks[3], (L, N_MOD * D_MODEL), 0.02),
        "norm1_g": 1.0 + nrm(ks[4], (L, D_MODEL), 0.05),
        "w_in": nrm(ks[5], (L, D_MODEL, D_IN), D_MODEL ** -0.5),
        "b_in": nrm(ks[6], (L, D_IN), 0.02),
        "a_ln_g": 1.0 + nrm(ks[7], (L, D_A), 0.05),
        "a_ln_b": nrm(ks[8], (L, D_A), 0.02),
        "a_spatial_w": nrm(ks[9], (L, N_HEADS_A, CHUNK, CHUNK), CHUNK ** -0.5),
        "a_spatial_b": 1.0 + nrm(ks[10], (L, N_HEADS_A, CHUNK), 0.1),
        "b_conv_w": nrm(ks[11], (L, CONV_WIDTH, D_B), CONV_WIDTH ** -0.5),
        "b_conv_b": nrm(ks[12], (L, D_B), 0.02),
        "b_gn_g": 1.0 + nrm(ks[13], (L, D_B), 0.05),
        "b_gn_b": nrm(ks[14], (L, D_B), 0.02),
        "out_norm_a_g": 1.0 + nrm(ks[15], (L, D_A), 0.05),
        "out_norm_b_g": 1.0 + nrm(ks[16], (L, D_B), 0.05),
        "w_out": nrm(ks[17], (L, D_MIX, D_MODEL), D_MIX ** -0.5),
        "norm2_g": 1.0 + nrm(ks[18], (L, D_MODEL), 0.05),
        "w_ffn_in": nrm(ks[19], (L, D_MODEL, 2 * D_FF), D_MODEL ** -0.5),
        "w_ffn_out": nrm(ks[20], (L, D_FF, D_MODEL), D_FF ** -0.5),
        "ada_f_w": nrm(ks[21], (D_MODEL, 2 * D_MODEL), D_MODEL ** -0.5),
        "ada_f_b": nrm(ks[22], (2 * D_MODEL,), 0.02),
        "norm_f_g": 1.0 + nrm(ks[23], (D_MODEL,), 0.05),
    }

def first_block(x, c, ada_w, ada_b, norm1_g, w_in, b_in, a_ln_g, a_ln_b, a_spatial_w,
              a_spatial_b, b_conv_w, b_conv_b, b_gn_g, b_gn_b, out_norm_a_g, out_norm_b_g,
              w_out, norm2_g, w_ffn_in, w_ffn_out, ada_f_w, ada_f_b, norm_f_g):
    c_act = jax.nn.silu(c)
    for i in range(DEPTH):
        cond = c_act @ ada_w[i] + ada_b[i]
        shift1, scale1, gate1, shift2, scale2, gate2 = jnp.split(cond, N_MOD, axis=-1)

        h = modulate(rmsnorm(x, norm1_g[i]), shift1, scale1)
        z = h @ w_in[i] + b_in[i]
        u, v, val, gate = jnp.split(z, [D_A, 2 * D_A, 2 * D_A + D_B], axis=-1)
        y_a = spatial_gating_mixer(jax.nn.gelu(u, approximate=False),
                                   jax.nn.gelu(v, approximate=False),
                                   a_ln_g[i], a_ln_b[i], a_spatial_w[i], a_spatial_b[i])
        y_b = conformer_conv_mixer(val, gate, b_conv_w[i], b_conv_b[i], b_gn_g[i], b_gn_b[i])
        y = jnp.concatenate([rmsnorm(y_a, out_norm_a_g[i]), rmsnorm(y_b, out_norm_b_g[i])], axis=-1)
        x = x + gate1[:, None, :] * (y @ w_out[i])

        h2 = modulate(rmsnorm(x, norm2_g[i]), shift2, scale2)
        g_ff, up_ff = jnp.split(h2 @ w_ffn_in[i], 2, axis=-1)
        x = x + gate2[:, None, :] * ((jax.nn.silu(g_ff) * up_ff) @ w_ffn_out[i])

    shift_f, scale_f = jnp.split(c_act @ ada_f_w + ada_f_b, 2, axis=-1)
    return modulate(rmsnorm(x, norm_f_g), shift_f, scale_f)


DEPTH_2 = 2

HEAD_DIM = 64
FOX_HEADS = 8
NSA_HEADS = 8
NSA_KV_GROUPS = 2
NSA_GROUP_SIZE = NSA_HEADS // NSA_KV_GROUPS
CMP_BLOCK = 32
CMP_STRIDE = 16
SLC_BLOCK = 64
N_SELECT = 16
WINDOW = 512
Q_BLOCK = 128
POOL_WINDOWS = (2, 4, 8, 16)
POOL_GROUP = D_MODEL // len(POOL_WINDOWS)
FFN_HIDDEN = -(-8 * D_MODEL // (3 * 256)) * 256
RMS_EPS = 1e-6
NEG_INF = -1e30
BIG = 1e30
N_EVEN = (DEPTH_2 + 1) // 2
N_ODD = DEPTH_2 // 2
MIX_WIDTH = (FOX_HEADS + NSA_HEADS) * HEAD_DIM
KV_DIM = NSA_KV_GROUPS * HEAD_DIM
IN_SIZES = (FOX_HEADS * HEAD_DIM, FOX_HEADS * HEAD_DIM, FOX_HEADS * HEAD_DIM, FOX_HEADS,
            NSA_HEADS * HEAD_DIM, KV_DIM, KV_DIM, KV_DIM, KV_DIM, KV_DIM, KV_DIM, 3 * NSA_HEADS)
IN_COLS = sum(IN_SIZES)


def rmsnorm_2(x, g):
    xf = x.astype(jnp.float32)
    y = xf * lax.rsqrt(jnp.mean(xf * xf, axis=-1, keepdims=True) + RMS_EPS)
    return (y * g.astype(jnp.float32)).astype(x.dtype)

def masked_softmax(s, mask):
    s = jnp.where(mask, s, NEG_INF)
    m = jnp.max(s, axis=-1, keepdims=True)
    e = jnp.where(mask, jnp.exp(s - m), 0.0)
    return e / jnp.maximum(jnp.sum(e, axis=-1, keepdims=True), 1e-30)

def alibi_slopes(n):
    return jnp.asarray(2.0 ** (-8.0 * (np.arange(n, dtype=np.float32) + 1.0) / n), dtype=jnp.float32)

def fox_attention(q, k, v, log_f):
    B, S, H, dh = q.shape
    c = jnp.transpose(jnp.cumsum(log_f, axis=1), (0, 2, 1))
    kpos = jnp.arange(S)
    scale = dh ** -0.5

    def block(qb):
        start = qb * Q_BLOCK
        t = start + jnp.arange(Q_BLOCK)
        qi = lax.dynamic_slice_in_dim(q, start, Q_BLOCK, axis=1)
        ci = lax.dynamic_slice_in_dim(c, start, Q_BLOCK, axis=2)
        s = jnp.einsum('bqhd,bkhd->bhqk', qi, k).astype(jnp.float32) * scale
        s = s + ci[..., None] - c[:, :, None, :]
        mask = kpos[None, :] <= t[:, None]
        p = masked_softmax(s, mask)
        return jnp.einsum('bhqk,bkhd->bqhd', p.astype(v.dtype), v)

    out = lax.map(block, jnp.arange(S // Q_BLOCK))
    return jnp.transpose(out, (1, 0, 2, 3, 4)).reshape(B, S, H * dh)

def nsa_compress(tok, pe, w1, w2):
    B, S, G, dh = tok.shape
    r = CMP_BLOCK // CMP_STRIDE
    n_chunks = S // CMP_STRIDE
    n_c = n_chunks - r + 1
    chunks = tok.reshape(B, n_chunks, CMP_STRIDE, G, dh)
    blocks = jnp.concatenate([chunks[:, j:j + n_c] for j in range(r)], axis=2)
    blocks = blocks + pe[None, None, :, None, :]
    flat = jnp.transpose(blocks, (0, 1, 3, 2, 4)).reshape(B, n_c, G, CMP_BLOCK * dh)
    return jax.nn.gelu(flat @ w1) @ w2

def nsa_attention(q, k_c, v_c, k_s, v_s, k_w, v_w, gates, pe, w1, w2):
    B, S, H, dh = q.shape
    G = k_c.shape[2]
    R = H // G
    scale = dh ** -0.5
    slopes = alibi_slopes(H).reshape(G, R)
    dt = q.dtype
    r = CMP_BLOCK // CMP_STRIDE
    ratio = SLC_BLOCK // CMP_STRIDE
    n_s = S // SLC_BLOCK
    n_sel = min(N_SELECT, n_s)

    kc = nsa_compress(k_c, pe[0], w1[0], w2[0])
    vc = nsa_compress(v_c, pe[1], w1[1], w2[1])
    n_c = kc.shape[1]
    cmp_end = jnp.arange(n_c) * CMP_STRIDE + CMP_BLOCK - 1

    q_g = q.reshape(B, S, G, R, dh)
    k_blocks = jnp.transpose(k_s.reshape(B, n_s, SLC_BLOCK, G, dh), (0, 3, 1, 2, 4)).reshape(B, G, n_s, SLC_BLOCK * dh)
    v_blocks = jnp.transpose(v_s.reshape(B, n_s, SLC_BLOCK, G, dh), (0, 3, 1, 2, 4)).reshape(B, G, n_s, SLC_BLOCK * dh)
    k_w_pad = jnp.pad(k_w, ((0, 0), (WINDOW, 0), (0, 0), (0, 0)))
    v_w_pad = jnp.pad(v_w, ((0, 0), (WINDOW, 0), (0, 0), (0, 0)))
    blk = jnp.arange(n_s)

    def block(qb):
        start = qb * Q_BLOCK
        t = start + jnp.arange(Q_BLOCK)
        tf = t.astype(jnp.float32)
        qi = lax.dynamic_slice_in_dim(q_g, start, Q_BLOCK, axis=1)
        gi = lax.dynamic_slice_in_dim(gates, start, Q_BLOCK, axis=1)

        d_c = tf[:, None] - cmp_end[None, :].astype(jnp.float32)
        s_c = jnp.einsum('bqgrd,bngd->bgrqn', qi, kc).astype(jnp.float32) * scale
        s_c = s_c - slopes[None, :, :, None, None] * d_c
        p_c = masked_softmax(s_c, d_c >= 0)
        o_c = jnp.einsum('bgrqn,bngd->bqgrd', p_c.astype(dt), vc)

        imp = jnp.sum(p_c, axis=2)
        imp = jnp.pad(imp, ((0, 0), (0, 0), (0, 0), (r - 1, ratio * n_s + r - 1 - n_c - (r - 1))))
        p_slc = imp[..., 0:ratio * n_s:ratio]
        for o in range(1, ratio + r - 1):
            p_slc = p_slc + imp[..., o:o + ratio * n_s:ratio]
        cur = t // SLC_BLOCK
        forced = (blk[None, :] == 0) | (blk[None, :] == cur[:, None]) | (blk[None, :] == cur[:, None] - 1)
        future = blk[None, :] > cur[:, None]
        p_slc = jnp.where(forced, BIG, jnp.where(future, NEG_INF, p_slc))
        _, idx = lax.top_k(p_slc, n_sel)

        flat_idx = idx.reshape(B, G, Q_BLOCK * n_sel)[..., None]
        kg = jnp.take_along_axis(k_blocks, flat_idx, axis=2).reshape(B, G, Q_BLOCK, n_sel * SLC_BLOCK, dh)
        vg = jnp.take_along_axis(v_blocks, flat_idx, axis=2).reshape(B, G, Q_BLOCK, n_sel * SLC_BLOCK, dh)
        kpos = (idx[..., None] * SLC_BLOCK + jnp.arange(SLC_BLOCK)).reshape(B, G, Q_BLOCK, n_sel * SLC_BLOCK)
        d_s = (t[None, None, :, None] - kpos).astype(jnp.float32)
        s_s = jnp.einsum('bqgrd,bgqkd->bgrqk', qi, kg).astype(jnp.float32) * scale
        s_s = s_s - slopes[None, :, :, None, None] * d_s[:, :, None]
        p_s = masked_softmax(s_s, (d_s >= 0)[:, :, None])
        o_s = jnp.einsum('bgrqk,bgqkd->bqgrd', p_s.astype(dt), vg)

        kw = lax.dynamic_slice_in_dim(k_w_pad, start, WINDOW + Q_BLOCK, axis=1)
        vw = lax.dynamic_slice_in_dim(v_w_pad, start, WINDOW + Q_BLOCK, axis=1)
        wpos = start - WINDOW + jnp.arange(WINDOW + Q_BLOCK)
        d_w = t[:, None] - wpos[None, :]
        m_w = (d_w >= 0) & (d_w < WINDOW) & (wpos[None, :] >= 0)
        s_w = jnp.einsum('bqgrd,bkgd->bgrqk', qi, kw).astype(jnp.float32) * scale
        s_w = s_w - slopes[None, :, :, None, None] * d_w.astype(jnp.float32)
        p_w = masked_softmax(s_w, m_w)
        o_w = jnp.einsum('bgrqk,bkgd->bqgrd', p_w.astype(dt), vw)

        return gi[..., 0:1] * o_c + gi[..., 1:2] * o_s + gi[..., 2:3] * o_w

    out = lax.map(block, jnp.arange(S // Q_BLOCK))
    return jnp.transpose(out, (1, 0, 2, 3, 4, 5)).reshape(B, S, H * dh)

def mixer_fox_nsa(h, w_in, b_f, cmp_pe, cmp_w1, cmp_w2, w_out):
    B, S, _ = h.shape
    proj = h @ w_in
    offs = [0]
    for n in IN_SIZES:
        offs.append(offs[-1] + n)
    fq, fk, fv, ff, nq, kc, vc, ks, vs, kw, vw, ng = [proj[..., offs[i]:offs[i + 1]] for i in range(len(IN_SIZES))]
    hd = (B, S, FOX_HEADS, HEAD_DIM)
    log_f = jax.nn.log_sigmoid((ff + b_f).astype(jnp.float32))
    o_fox = fox_attention(fq.reshape(hd), fk.reshape(hd), fv.reshape(hd), log_f)
    kvd = (B, S, NSA_KV_GROUPS, HEAD_DIM)
    gates = jax.nn.sigmoid(ng.astype(jnp.float32)).astype(h.dtype).reshape(B, S, NSA_KV_GROUPS, NSA_GROUP_SIZE, 3)
    o_nsa = nsa_attention(nq.reshape(B, S, NSA_HEADS, HEAD_DIM), kc.reshape(kvd), vc.reshape(kvd),
                          ks.reshape(kvd), vs.reshape(kvd), kw.reshape(kvd), vw.reshape(kvd),
                          gates, cmp_pe, cmp_w1, cmp_w2)
    return jnp.concatenate([o_fox, o_nsa], axis=-1) @ w_out

def mixer_pool(h, w_groups, scale):
    B, S, D = h.shape
    hf = h.astype(jnp.float32)
    c = jnp.cumsum(hf, axis=1)
    count = jnp.arange(1, S + 1, dtype=jnp.float32)
    outs = []
    for gi, w in enumerate(POOL_WINDOWS):
        sl = slice(gi * POOL_GROUP, (gi + 1) * POOL_GROUP)
        cg = c[..., sl]
        lag = jnp.pad(cg, ((0, 0), (w, 0), (0, 0)))[:, :S]
        mean = (cg - lag) / jnp.minimum(count, float(w))[None, :, None]
        outs.append(mean - hf[..., sl])
    pooled = jnp.stack(outs, axis=2).astype(h.dtype)
    y = jnp.einsum('bsgc,gcd->bsgd', pooled, w_groups).reshape(B, S, D)
    return y * scale

def swiglu(h, w_gate, w_up, w_down):
    return (jax.nn.silu(h @ w_gate) * (h @ w_up)) @ w_down

def second_inputs(seed: int = 0) -> dict:
    key = jax.random.key(seed)
    ks = jax.random.split(key, 13)
    f32 = jnp.float32
    dh = HEAD_DIM
    x = jax.random.normal(ks[0], (BATCH, SEQ, D_MODEL), f32)
    norm_g = 1.0 + 0.05 * jax.random.normal(ks[1], (DEPTH_2, 4, D_MODEL), f32)
    attn_w_in = jax.random.normal(ks[2], (N_EVEN, D_MODEL, IN_COLS), f32) * D_MODEL ** -0.5
    fox_b_f = jax.random.uniform(ks[3], (N_EVEN, FOX_HEADS), f32, 1.0, 4.0)
    nsa_cmp_pe = 0.1 * jax.random.normal(ks[4], (N_EVEN, 2, CMP_BLOCK, dh), f32)
    nsa_cmp_w1 = jax.random.normal(ks[5], (N_EVEN, 2, CMP_BLOCK * dh, dh), f32) * (CMP_BLOCK * dh) ** -0.5
    nsa_cmp_w2 = jax.random.normal(ks[6], (N_EVEN, 2, dh, dh), f32) * dh ** -0.5
    attn_w_out = jax.random.normal(ks[7], (N_EVEN, MIX_WIDTH, D_MODEL), f32) * MIX_WIDTH ** -0.5
    pool_w = jax.random.normal(ks[8], (N_ODD, len(POOL_WINDOWS), POOL_GROUP, POOL_GROUP), f32) * POOL_GROUP ** -0.5
    pool_scale = 1.0 + 0.1 * jax.random.normal(ks[9], (N_ODD, D_MODEL), f32)
    ffn_w_gate = jax.random.normal(ks[10], (DEPTH_2, D_MODEL, FFN_HIDDEN), f32) * D_MODEL ** -0.5
    ffn_w_up = jax.random.normal(ks[11], (DEPTH_2, D_MODEL, FFN_HIDDEN), f32) * D_MODEL ** -0.5
    ffn_w_down = jax.random.normal(ks[12], (DEPTH_2, FFN_HIDDEN, D_MODEL), f32) * FFN_HIDDEN ** -0.5
    return {"x": x, "norm_g": norm_g, "attn_w_in": attn_w_in, "fox_b_f": fox_b_f,
            "nsa_cmp_pe": nsa_cmp_pe, "nsa_cmp_w1": nsa_cmp_w1, "nsa_cmp_w2": nsa_cmp_w2,
            "attn_w_out": attn_w_out, "pool_w": pool_w, "pool_scale": pool_scale,
            "ffn_w_gate": ffn_w_gate, "ffn_w_up": ffn_w_up, "ffn_w_down": ffn_w_down}

def second_block(x, norm_g, attn_w_in, fox_b_f, nsa_cmp_pe, nsa_cmp_w1, nsa_cmp_w2, attn_w_out,
              pool_w, pool_scale, ffn_w_gate, ffn_w_up, ffn_w_down):
    h = x
    for layer in range(DEPTH_2):
        g = norm_g[layer]
        i = layer // 2
        u = rmsnorm_2(h, g[0])
        if layer % 2 == 0:
            m = mixer_fox_nsa(u, attn_w_in[i], fox_b_f[i], nsa_cmp_pe[i], nsa_cmp_w1[i], nsa_cmp_w2[i], attn_w_out[i])
        else:
            m = mixer_pool(u, pool_w[i], pool_scale[i])
        h = h + rmsnorm_2(m, g[1])
        u = rmsnorm_2(h, g[2])
        h = h + rmsnorm_2(swiglu(u, ffn_w_gate[layer], ffn_w_up[layer], ffn_w_down[layer]), g[3])
    return h


def setup_inputs(seed=0):
    out = dict(first_inputs(seed))
    for name, value in second_inputs(seed + 1).items():
        if name != "x":
            out[name + "_2"] = value
    return out


def reference(
    x, c, ada_w, ada_b, norm1_g, w_in, b_in, a_ln_g, a_ln_b, a_spatial_w, a_spatial_b, b_conv_w,
    b_conv_b, b_gn_g, b_gn_b, out_norm_a_g, out_norm_b_g, w_out, norm2_g, w_ffn_in, w_ffn_out,
    ada_f_w, ada_f_b, norm_f_g, norm_g_2, attn_w_in_2, fox_b_f_2, nsa_cmp_pe_2, nsa_cmp_w1_2,
    nsa_cmp_w2_2, attn_w_out_2, pool_w_2, pool_scale_2, ffn_w_gate_2, ffn_w_up_2, ffn_w_down_2,
):
    x = first_block(
        x, c, ada_w, ada_b, norm1_g, w_in, b_in, a_ln_g, a_ln_b, a_spatial_w, a_spatial_b,
        b_conv_w, b_conv_b, b_gn_g, b_gn_b, out_norm_a_g, out_norm_b_g, w_out, norm2_g,
        w_ffn_in, w_ffn_out, ada_f_w, ada_f_b, norm_f_g,
    )
    return second_block(
        x, norm_g_2, attn_w_in_2, fox_b_f_2, nsa_cmp_pe_2, nsa_cmp_w1_2, nsa_cmp_w2_2,
        attn_w_out_2, pool_w_2, pool_scale_2, ffn_w_gate_2, ffn_w_up_2, ffn_w_down_2,
    )


_drawn_inputs = setup_inputs


def setup_inputs(seed=0):
    import zlib

    import numpy as np

    out = dict(_drawn_inputs(seed))
    spreads = {}
    factors = {'b_in': 4.644, 'a_ln_g': 4.483, 'a_ln_b': 8.0, 'b_conv_b': 4.27, 'b_gn_b': 6.684}
    for name, (base, spread) in spreads.items():
        noise = np.random.default_rng([zlib.crc32(name.encode()), seed]).standard_normal(out[name].shape)
        drawn = base * np.exp(spread * noise) if base else spread * noise
        out[name] = __import__('jax').numpy.asarray(drawn.astype(out[name].dtype))
    for name, factor in factors.items():
        out[name] = (out[name] * factor).astype(out[name].dtype)
    return out
```

```python
from contextlib import ExitStack

import numpy as np

import concourse.bass as bass
from concourse import mybir

F32 = mybir.dt.float32
F32R = mybir.dt.float32r
ALU = mybir.AluOpType
ACT = mybir.ActivationFunctionType

P = 128
S = 512
D = 1024
C = D // P
TC = S // P
DA = D // 2
CA = DA // P
HA = 8
GB = 8
TAPS = 31
FF = 2816
CF = FF // P
KH = CF // 2
NH = 8
DH = 64
NCMP = (S // 16) - 1
CMPB = 32
EPS = 1e-6
NEG = -1e30

_SIZES = [("c", 8), ("ada_b", 64), ("norm1", 8), ("norm2", 8), ("normf", 8), ("b_in", 16), ("gn_g", 4),
          ("gn_b", 4), ("conv_b", 4), ("conv_w", 4 * TAPS), ("on_a", 4), ("on_b", 4), ("norm_g2", 64),
          ("pool_s", 8)]
COL = {}
_at = 0
for _n, _w in _SIZES:
    COL[_n] = _at
    _at += _w
NVEC = _at

R_ADA, R_P1 = 0, 4
G = {"w_out": 2, "ffi0": 11, "ffo0": 4, "att5": 2, "att6": 4, "att_out": 2, "ffi1": 11, "ffo1": 4,
     "pool": 1, "ffi2": 11, "ffo2": 4}
ROUND, N0, O0 = {}, {}, {}
_r, _b, _o = R_P1 + 16, 16, 2 + 16
for _n in ("w_out", "ffi0", "ffo0", "att5", "att6", "att_out", "ffi1", "ffo1", "pool", "ffi2", "ffo2"):
    ROUND[_n], N0[_n], O0[_n] = _r, _b, _o
    _r += G[_n]
    _b += 0 if _n == "pool" else 4 * G[_n]
    _o += 8 if _n == "pool" else (2 if _n.startswith("ffo") else 4) * G[_n]


def build_program(nc, xT, vec, ada_w, w_in, w_out, ffi, ffo, ln_rows, ws, bs, att_w, att_out, bf, pe, w1, w2,
                  pool_w, f2i, f2o, outT):
    ctx = ExitStack()
    with ctx:
        def sb(name, shape, dt=F32):
            return ctx.enter_context(nc.sbuf_tensor(name, shape, dt))

        def sem(name):
            return ctx.enter_context(nc.semaphore(name))

        RAW = [sb(f"raw{i}", [P, KH * P]) for i in range(4)]
        WH = [sb(f"w_hi{i}", [P, KH * P], F32R) for i in range(2)]
        WL = [sb(f"w_lo{i}", [P, KH * P], F32R) for i in range(2)]
        X = sb("x_res", [P, C, S])
        HH = sb("h_hi", [P, C, S], F32R)
        HL = sb("h_lo", [P, C, S], F32R)
        TMP = sb("tmp", [P, 2, S])
        TMP2 = sb("tmp2", [P, 2, S])
        VEC = sb("vec_sb", [P, NVEC])
        MOD = sb("mod", [P, 64])
        GS = sb("gs", [P, 3, C])
        PG = sb("pool_gs", [P, C])
        CACT = sb("c_act", [P, C])
        IDN = sb("ident", [P, P])
        ONE = sb("ones", [P, P])
        STAT = sb("stat", [P, 16])
        NHALF = sb("nhalf", [P, 4])
        ACC = TMP2[:, 0, :]
        DG = TMP2[:, 1, :]
        LX, LA, LE, NG = TMP[0:NH, 0, :], TMP[0:NH, 1, :], TMP2[0:NH, 0, :], TMP2[0:3 * NH, 1, :]
        PS = [ctx.enter_context(nc.psum_tensor(f"bank{i}", [P, S], F32)) for i in range(8)]
        NS, RB, ADA = PS[6], PS[7], PS[5]

        with ExitStack() as life:
            def lb(name, shape, dt=F32):
                return life.enter_context(nc.sbuf_tensor(name, shape, dt))
            U = lb("u_act", [P, CA, S])
            V = lb("v_act", [P, CA, S])
            Y = lb("y_pad", [P, CA, S + TAPS - 1])
            SIG = lb("sig", [P, S])
            CV = lb("conv", [P, CA, S])
            VT = lb("v_tok", [P, TC, DA])
            LNR = lb("ln_rows_sb", [P, 2, DA])
            WS = lb("ws_sb", [P, HA, P])
            BS = lb("bs_sb", [P, CA, P])
            YA = lb("ya", [P, CA, S])
            GD = lb("gd", [P, P])
            GSEL = lb("gsel", [P, 2])
            SELG = lb("selg", [GB, CA, P])
            BN = lb("bn", [P, TC, 6])
            MV = lb("mv", [P, TC, 2])
            R32 = lb("r32", [P, 3, 32])
            R8 = lb("r8", [GB, S])
        with ExitStack() as life:
            def lb2(name, shape, dt=F32):
                return life.enter_context(nc.sbuf_tensor(name, shape, dt))
            with ExitStack() as sub:
                W1B = sub.enter_context(nc.sbuf_tensor("w1b", [P, 2, CMPB, P], F32))
            AH = lb2("ao_hi", [P, C, S], F32R)
            AL = lb2("ao_lo", [P, C, S], F32R)
            W2B = lb2("w2b", [P, 2, P])
            PEB = lb2("peb", [P, 2, CMPB])
            BF = lb2("bf_sb", [NH, 1])
            LF = lb2("log_f_sum", [NH, S])
            CTK = lb2("c_tok", [P, TC, NH])
            GT = lb2("g_tok", [P, TC, 3 * NH])
            with ExitStack() as sub:
                KE = sub.enter_context(nc.sbuf_tensor("ke", [P, 2, NCMP, CMPB], F32))
            FB = lb2("fox_bias", [P, 2, 10 * P])
            G1 = lb2("g1", [P, 2, NCMP])
            KCF = lb2("kcf", [P, 2, NCMP])
            VCT = lb2("vct", [NCMP, P])
            KS = lb2("k_slc", [P, S])
            KW = lb2("k_win", [P, S])
            VF = lb2("vf", [P, S])
            VST = lb2("v_slc_tok", [P, TC, P])
            VWT = lb2("v_win_tok", [P, TC, P])
            FQ = lb2("fq", [P, S])
            FK = lb2("fk", [P, S])
            NQ = lb2("nq", [P, S])
            FVT = lb2("fv_tok", [P, TC, P])
            CSEL = lb2("c_sel", [NH, 2, S])
            DM = lb2("dist", [P, S])
            DC = lb2("dist_cmp", [P, TC, NCMP])
            CM = lb2("mask_cmp", [P, TC, NCMP])
            ALB = lb2("alibi", [P, 2, S])
            CLB = lb2("alibi_cmp", [P, 2, TC, NCMP])
            SL = lb2("slopes", [P, NH])
            CTS = lb2("c_tok_it", [P, TC, 2])
            GTS = lb2("g_it", [P, TC, 2, 4])
            SC = lb2("scores", [P, 8, S])
            PT = lb2("p_t", [P, 3, S])
            AST = lb2("att_stat", [P, 3, 32])
        with ExitStack() as life:
            def lb3(name, shape, dt=F32):
                return life.enter_context(nc.sbuf_tensor(name, shape, dt))
            FH = lb3("hid_hi", [P, CF, S], F32R)
            FL = lb3("hid_lo", [P, CF, S], F32R)
            M = lb3("m_out", [P, C, S])
        with ExitStack() as life:
            PUT = life.enter_context(nc.sbuf_tensor("pool_u", [P, C, S], F32))
            PCS = life.enter_context(nc.sbuf_tensor("pool_cs", [P, 2, S + 16], F32))
            PINV = life.enter_context(nc.sbuf_tensor("pool_inv", [P, 4, S], F32))
            PIN = life.enter_context(nc.sbuf_tensor("pool_in", [P, C, S], F32))
            PTM = life.enter_context(nc.sbuf_tensor("pool_tmp", [P, 2, S], F32))

        ld = [sem(f"raw_loaded{i}") for i in range(4)]
        whi, wlo, mm = sem("w_hi_ready"), sem("w_lo_ready"), sem("block_multiplied")
        ev = [sem(f"bank{i}_evacuated") for i in range(2)]
        raw_used = sem("raw_block_used")
        ld_x, ld_vec, ld_ln, ld_ws, ld_bs, ld_att = (sem(n) for n in (
            "x_loaded", "vec_loaded", "ln_loaded", "ws_loaded", "bs_loaded", "att_const_loaded"))
        const_ready, pool_chain, c_ready, mod_ready = (sem(n) for n in (
            "const_ready", "pool_chain", "c_ready", "mod_ready"))
        store_done = sem("store_done")
        wait_held = sem("wait_held")
        x_ready = sem("x_final")

        n_ms = sem("norm_mean_square")
        n_rs = sem("norm_power")
        n_dg = sem("norm_diagonal")
        n_rb = sem("norm_broadcast")

        n_sq = sem("norm_squares")
        n_used = sem("norm_squares_summed")
        n_acc = sem("norm_running_sum")
        n_t = sem("normed_chunk")
        n_hi = sem("normed_chunk_hi")
        n_lo = sem("normed_chunk_lo")

        class Norm:
            def __init__(self, count, at):
                self.count = count
                self.sq, self.used, self.acc, self.t, self.hi, self.lo = at

        kinds = (("n1", C, C, 0, C, C, C), ("na", CA, CA, 0, CA, CA, CA), ("nb", CA, CA, 0, CA, CA, CA),
                 ("n2", C, 1, C + 1, C, C, C), ("nf", C, 1, C + 1, C, 0, 0), ("q0", C, C, 0, C, C, C),
                 ("r1", 0, 1, C + 1, C, 0, 0), ("q1", C, C, 0, C, C, C), ("r2", 0, 1, C + 1, C, 0, 0),
                 ("q2", C, C, 0, 0, 0, 0), ("r3", 0, 1, C + 1, C, 0, 0), ("q3", C, C, 0, C, C, C),
                 ("r4", 0, 1, C + 1, C, 0, 0))
        nj, at = {}, [0] * 6
        for q, (k, *counts) in enumerate(kinds):
            nj[k] = Norm(q + 1, at)
            at = [a + b for a, b in zip(at, counts)]

        def split_hi(n, par, s, kc, rnd, first=False):
            nc.scalar.wait_ge(ld[s], 16 * (rnd + 1))
            if not first:
                nc.scalar.wait_ge(mm, n - 1)
            nc.scalar.activation(WH[par][:, 0:kc * P], RAW[s][:, 0:kc * P], ACT.Copy).then_inc(whi, 1)

        def split_lo(n, par, s, kc):
            nc.vector.wait_ge(whi, n + 1)
            nc.vector.tensor_tensor(WL[par][:, 0:kc * P], RAW[s][:, 0:kc * P],
                                    WH[par][:, 0:kc * P].bitcast(F32), ALU.subtract).then_inc(wlo, 1)

        def groups(eng, count, uniform, body):
            n = count if uniform else count - 1
            if n:
                with eng.Fori(0, n) as g:
                    body(g, False)
            if not uniform:
                body(count - 1, True)

        def follow(name):
            return {"w_out": (C, ROUND["ffi0"]), "ffi0": (KH, ROUND["ffo0"]), "ffo0": (C, ROUND["att5"]),
                    "att5": (C, ROUND["att6"]), "att6": (C, ROUND["att_out"]), "att_out": (C, ROUND["ffi1"]),
                    "ffi1": (KH, ROUND["ffo1"]), "ffo1": None, "ffi2": (KH, ROUND["ffo2"]), "ffo2": None}[name]

        def kc_of(name):
            return KH if name.startswith("ffo") else C

        def phase_splits(name, eng, step, evac):
            kc, nxt = kc_of(name), follow(name)
            uniform = nxt is not None and nxt[0] == kc

            def body(g, last):
                for t in range(4):
                    n = N0[name] + 4 * g + t
                    if t < 2:
                        step(n + 2, t % 2, t + 2, kc, ROUND[name] + g)
                    elif not last:
                        step(n + 2, t % 2, t - 2, kc, ROUND[name] + g + 1)
                    elif nxt is not None:
                        step(n + 2, t % 2, t - 2, nxt[0], nxt[1])
                    evac(g, t)
            groups(eng, G[name], uniform, body)

        def act_step(n, par, s, kc, rnd):
            split_hi(n, par, s, kc, rnd)

        def dve_step(n, par, s, kc, rnd):
            split_lo(n, par, s, kc)

        def block(n, par, kc, hi, lo, k0, bank, start, stop, ready=None):
            pe_ = nc.tensor
            pe_.wait_ge(wlo, n + 1)
            for k in range(kc):
                if ready is not None:
                    pe_.wait_ge(n_lo, ready + k + 1)
                w_h, w_l = WH[par][:, k * P:(k + 1) * P], WL[par][:, k * P:(k + 1) * P]
                pe_.matmul(bank[:, :], w_h, hi[:, k0 + k, :], start=start and k == 0, stop=False)
                pe_.matmul(bank[:, :], w_h, lo[:, k0 + k, :], start=False, stop=False)
                last = pe_.matmul(bank[:, :], w_l, hi[:, k0 + k, :], start=False, stop=stop and k == kc - 1)
            last.then_inc(mm, 1)

        def pe_phase(name, hi, lo, ready):
            with nc.tensor.Fori(0, G[name]) as g:
                for t in range(4):
                    nc.tensor.wait_ge(ev[t % 2], O0[name] // 2 + 2 * g + t // 2)
                    block(N0[name] + 4 * g + t, t % 2, C, hi, lo, 0, PS[t % 2], True, True,
                          ready if t == 0 else None)

        def pe_down(name, hid_ready):
            with nc.tensor.Fori(0, G[name]) as g:
                for t in range(4):
                    if t % 2 == 0:
                        nc.tensor.wait_ge(ev[t // 2], O0[name] // 2 + g)
                    nc.tensor.wait_ge(hid_ready, KH * (t % 2 + 1))
                    block(N0[name] + 4 * g + t, t % 2, KH, FH, FL, KH * (t % 2), PS[t // 2],
                          t % 2 == 0, t % 2 == 1)

        def pe_sum_direct(nj_, K, ring):
            for k in range(K):
                nc.tensor.wait_ge(n_sq, nj_.sq + k + 1)
                for i in range(TC):
                    m = nc.tensor.matmul(NS[:, i:i + 1], ring[:, k % 2, i * P:(i + 1) * P], ONE[:, 0:1],
                                         start=(k == 0 and i == 0), stop=(k == K - 1), skip_group_check=True)
                m.then_inc(n_used, 1)

        def pe_sum_acc(nj_, K):
            nc.tensor.wait_ge(n_acc, nj_.acc + K + 1)
            for i in range(TC):
                m = nc.tensor.matmul(NS[:, i:i + 1], ACC[:, i * P:(i + 1) * P], ONE[:, 0:1], start=True, stop=True)
            m.then_inc(n_used, 1)

        def pe_bcast(nj_):
            nc.tensor.wait_ge(n_dg, nj_.count)
            nc.tensor.matmul(RB[:, :], ONE[:, :], DG, start=True, stop=True).then_inc(n_rb, 1)

        def dve_diag(nj_, used, width):
            nc.vector.wait_ge(n_used, nj_.used + used)
            nc.vector.tensor_scalar(STAT[:, 0:4], NS[:, 0:4], 1.0 / width, EPS, ALU.mult, ALU.add).then_inc(n_ms, 1)
            nc.vector.wait_ge(n_rs, nj_.count)
            nc.vector.tensor_tensor(DG.rearrange("p (i t) -> p i t", i=TC),
                                    IDN[:, :].rearrange("p (i t) -> p i t", i=1).to_broadcast([P, TC, P]),
                                    STAT[:, 4:8].rearrange("p (i t) -> p i t", t=1).to_broadcast([P, TC, P]),
                                    ALU.mult).then_inc(n_dg, 1)

        def pool_rsqrt(nj_):
            nc.gpsimd.wait_ge(n_ms, nj_.count)
            nc.gpsimd.tensor_tensor(STAT[:, 4:8], STAT[:, 0:4], NHALF[:, 0:4], ALU.pow).then_inc(n_rs, 1)

        def act_squares(nj_, K, src, ready, ring):
            for k in range(K):
                ready(k)
                if k >= 2:
                    nc.scalar.wait_ge(n_used, nj_.used + k - 1)
                nc.scalar.activation(ring[:, k % 2, :], src(k), ACT.Square).then_inc(n_sq, 1)

        def act_parts(nj_, K, k0=0, shift=None):
            for k in range(K):
                nc.scalar.wait_ge(n_t, nj_.t + k + 1)
                if shift is None:
                    nc.scalar.activation(HH[:, k0 + k, :], TMP[:, k % 2, :], ACT.Copy).then_inc(n_hi, 1)
                else:
                    nc.scalar.activation(HH[:, k0 + k, :], TMP[:, k % 2, :], ACT.Identity,
                                         bias=shift(k)).then_inc(n_hi, 1)

        def dve_parts(nj_, K, src, gain, k0=0, shift=None):
            nc.vector.wait_ge(n_rb, nj_.count)

            def low(k):
                nc.vector.wait_ge(n_hi, nj_.hi + k + 1)
                hi = HH[:, k0 + k, :].bitcast(F32)
                if shift is None:
                    nc.vector.tensor_tensor(HL[:, k0 + k, :], TMP[:, k % 2, :], hi, ALU.subtract).then_inc(n_lo, 1)
                else:
                    nc.vector.scalar_tensor_tensor(HL[:, k0 + k, :], TMP[:, k % 2, :], shift(k), hi, ALU.add,
                                                   ALU.subtract).then_inc(n_lo, 1)
            for k in range(K):
                if k >= 2:
                    nc.vector.wait_ge(n_lo, nj_.lo + k - 1)
                nc.vector.scalar_tensor_tensor(TMP[:, k % 2, :], src(k), gain(k), RB[:, :], ALU.mult,
                                               ALU.mult).then_inc(n_t, 1)
                if k >= 1:
                    low(k - 1)
            low(K - 1)

        def vcol(name, k):
            return VEC[:, COL[name] + k:COL[name] + k + 1]

        def dve_clear_acc(nj_):
            nc.vector.memset(ACC, 0.0).then_inc(n_acc, 1)

        def dve_gated(nj_, name, m, b, gate0):
            cnt = O0[name] // 2
            nc.vector.wait_ge(mm, m[1])
            nc.vector.scalar_tensor_tensor(X[:, bass.ds(m[0], 1), :], PS[b][:, :].rearrange("p (a s) -> p a s", a=1),
                                           MOD[:, bass.ds(gate0 + m[0], 1)], X[:, bass.ds(m[0], 1), :],
                                           ALU.mult, ALU.add).then_inc(ev[b], 1)
            nc.vector.wait_ge(n_sq, nj_.sq + m[0] + 1)
            nc.vector.wait_ge(n_acc, nj_.acc + m[0] + 1)
            nc.vector.tensor_tensor(ACC, ACC, TMP[:, b, :], ALU.add).then_inc(n_acc, 1)

        def act_gated(nj_, name, m, b, half):
            nc.scalar.wait_ge(ev[b], O0[name] // 2 + half + 1)
            nc.scalar.activation(TMP[:, b:b + 1, :], X[:, bass.ds(m, 1), :], ACT.Square).then_inc(n_sq, 1)

        def act_m(nj_, name, m, b, done, gain, sqscale=None):
            nc.scalar.wait_ge(mm, done)
            nc.scalar.activation(M[:, bass.ds(m, 1), :], PS[b][:, :].rearrange("p (a s) -> p a s", a=1), ACT.Copy,
                                 scale=gain)
            nc.scalar.wait_ge(n_acc, nj_.acc + m)
            if sqscale is None:
                nc.scalar.activation(TMP[:, b, :], PS[b][:, :], ACT.Square).then_inc(ev[b], 1)
            else:
                nc.scalar.activation(TMP[:, b, :], PS[b][:, :], ACT.Square, scale=sqscale).then_inc(ev[b], 1)

        def dve_m(nj_, name, m, b, half):
            nc.vector.wait_ge(ev[b], O0[name] // 2 + half + 1)
            nc.vector.wait_ge(n_acc, nj_.acc + m + 1)
            nc.vector.tensor_tensor(ACC, ACC, TMP[:, b, :], ALU.add).then_inc(n_acc, 1)

        def dve_add_normed(nj_, xs):
            nc.vector.wait_ge(n_rb, nj_.count)

            def add(k):
                nc.vector.wait_ge(n_t, nj_.t + k + 1)
                nc.vector.tensor_tensor(X[:, k, :], X[:, k, :], TMP[:, k % 2, :], ALU.add).then_inc(xs, 1)
            for k in range(C):
                if k >= 2:
                    nc.vector.wait_ge(xs, k - 1)
                nc.vector.tensor_tensor(TMP[:, k % 2, :], M[:, k, :], RB[:, :], ALU.mult).then_inc(n_t, 1)
                if k >= 1:
                    add(k - 1)
            add(C - 1)

        ff = [{k: sem(f"ffn{j}_{k}") for k in ("hid_hi", "hid_lo")} for j in range(3)]
        xs = [sem(f"x_renewed{j}") for j in range(5)]

        def act_ffi(name, s, g, t):
            j, o = 2 * g + t // 2, O0[name] // 2 + 2 * g + t // 2
            if t % 2 == 0:
                nc.scalar.wait_ge(mm, N0[name] + 4 * g + t + 1)
                nc.scalar.activation(TMP[:, t // 2, :], PS[0][:, :], ACT.Silu).then_inc(ev[0], 1)
            else:
                nc.scalar.wait_ge(ev[1], o + 1)
                nc.scalar.activation(FH[:, bass.ds(j, 1), :], TMP2[:, t // 2:t // 2 + 1, :],
                                     ACT.Copy).then_inc(s["hid_hi"], 1)

        def dve_ffi(name, s, g, t):
            j, o = 2 * g + t // 2, O0[name] // 2 + 2 * g + t // 2
            if t % 2 == 1:
                nc.vector.wait_ge(mm, N0[name] + 4 * g + t + 1)
                nc.vector.wait_ge(ev[0], o + 1)
                nc.vector.wait_ge(wlo, N0[name] + 4 * g + t + 2)
                nc.vector.tensor_tensor(TMP2[:, t // 2, :], TMP[:, t // 2, :], PS[1][:, :],
                                        ALU.mult).then_inc(ev[1], 1)
                nc.vector.wait_ge(s["hid_hi"], j + 1)
                nc.vector.tensor_tensor(FL[:, bass.ds(j, 1), :], TMP2[:, t // 2:t // 2 + 1, :],
                                        FH[:, bass.ds(j, 1), :].bitcast(F32), ALU.subtract).then_inc(s["hid_lo"], 1)

        j1 = {k: sem("p1_" + k) for k in (
            "vt", "vtc", "bn", "bna", "msv", "rsv", "ln1", "ln", "conv", "gm", "xc", "sq", "var", "v32", "sd", "rc",
            "r8t", "r8", "gb", "gx", "yb", "sp", "ya1", "ya")}
        a5 = {k: sem("a5_" + k) for k in (
            "xf", "abs", "ex", "lnx", "lf", "cs", "ct", "ctc", "ngt", "ngc", "hc", "g1", "kc2", "kcf",
            "vcf", "vct", "vctc", "vt", "vtc")}
        a6 = {k: sem("a6_" + k) for k in (
            "csel", "cb", "fb", "fbm", "stg", "fvt", "fvc", "qk", "sc", "ex", "cm", "mx", "rc", "rg", "nm",
            "tr", "pt", "pv", "of", "oh", "ol")}
        p10 = {k: sem("p10_" + k) for k in ("u", "z", "cs", "d", "e", "in", "inv")}

        KIND = ("fox", "cmp", "slc", "win")

        def item(x):
            g, j = divmod(x, 4)
            i, half = divmod(g, 2)
            return KIND[j], i, half, (NCMP if j == 1 else (i + 1) * P)

        def foff(i):
            return (0, P, 3 * P, 6 * P)[i]

        blk = ctx.enter_context(nc.Block())

        @blk.sync
        def _(sp):
            sp.dma_start(VEC[:, :], vec).then_inc(ld_vec, 16)

            def load(s, src, width):
                sp.dma_start(RAW[s][:, 0:width], src).then_inc(ld[s], 16)

            for s in range(4):
                load(s, ada_w[s], C * P)
            sp.dma_start(X[:, :, :], xT).then_inc(ld_x, 16)
            with sp.Fori(1, 4) as r:
                for s in range(4):
                    sp.wait_ge(raw_used, 4 * (r - 1) + s + 1)
                    load(s, ada_w[bass.ds(4 * r + s, 1), :, :].rearrange("a p n -> (a p) n"), C * P)
            sp.wait_ge(raw_used, 13)
            load(0, w_in[0], C * P)
            for s in range(1, 4):
                sp.wait_ge(raw_used, 13 + s)
                load(s, ada_w[15 + s], C * P)
            sp.dma_start(LNR[:, :, :], ln_rows.rearrange("(o a) n -> o a n", o=1).to_broadcast([P, 2, DA])).then_inc(ld_ln, 16)
            sp.dma_start(WS[:, :, :], ws).then_inc(ld_ws, 16)
            for h in range(HA):
                half = h % 2
                sp.dma_start(BS[64 * half:64 * half + 64, h // 2, :], bs[h:h + 1, :].to_broadcast([64, P])).then_inc(ld_bs, 16)
            with sp.Fori(1, 16) as st:
                sp.wait_ge(wlo, st)
                load(0, w_in[bass.ds(st, 1), :, :].rearrange("a p n -> (a p) n"), C * P)
                for s in range(1, 4):
                    sp.wait_ge(raw_used, 3 * st + 13 + s)
                    load(s, ada_w[bass.ds(3 * st + 15 + s, 1), :, :].rearrange("a p n -> (a p) n"), C * P)

            def stream(name, src, width, base=0, first=0):
                with sp.Fori(first, G[name]) as g:
                    for s in range(4):
                        sp.wait_ge(wlo, N0[name] + 4 * g + s - 3)
                        load(s, src[bass.ds(base + 4 * g + s, 1), :, :].rearrange("a p n -> (a p) n"), width)

            sp.wait_ge(wlo, 16)
            load(0, w_out[0], C * P)
            for s in range(1, 4):
                sp.wait_ge(raw_used, 61 + s)
                load(s, w_out[s], C * P)
            stream("w_out", w_out, C * P, first=1)
            stream("ffi0", ffi, C * P)
            stream("ffo0", ffo, KH * P)
            stream("att5", att_w, C * P)
            stream("att6", att_w, C * P, base=8)
            stream("att_out", att_out, C * P)
            stream("ffi1", f2i, C * P)
            stream("ffo1", f2o, KH * P)
            for s in range(4):
                sp.wait_ge(wlo, N0["ffi2"] - 3 + s)
                load(s, pool_w[s], 4 * P)
            for s in range(4):
                sp.wait_ge(raw_used, 64 + s + 1)
                load(s, f2i[44 + s], C * P)
            stream("ffi2", f2i, C * P, base=44, first=1)
            stream("ffo2", f2o, KH * P, base=16)
            for k in range(C):
                sp.wait_ge(xs[4], k + 1)
                sp.dma_start(outT[:, k, :], X[:, k, :]).then_inc(store_done, 16)
            sp.wait_ge(store_done, 16 * C)

        @blk.gpsimd
        def _(pool):
            cnt = [0]

            def chain(ins):
                cnt[0] += 1
                ins.then_inc(pool_chain, 1)
                pool.wait_ge(pool_chain, cnt[0])

            chain(pool.memset(IDN[:, :], 0.0))
            chain(pool.affine_select(out=IDN[:, :], in_=IDN[:, :], compare_op=ALU.not_equal, fill=1.0, base=0,
                                     pattern=[[-1, P]], channel_multiplier=1))
            chain(pool.memset(NHALF[:, :], -0.5))
            chain(pool.memset(GD[:, :], 0.0))
            for h in range(2):
                chain(pool.memset(GD[64 * h:64 * h + 64, 64 * h:64 * h + 64], 1.0 / 64))
            chain(pool.memset(GSEL[:, :], 0.0))
            for h in range(2):
                chain(pool.memset(GSEL[64 * h:64 * h + 64, h:h + 1], 1.0 / 64))
            chain(pool.memset(SELG[:, :, :], 0.0))
            sg = SELG[:, :, :].rearrange("g c (h d) -> g c h d", h=2)
            chain(pool.affine_select(out=sg, in_=sg, compare_op=ALU.not_equal, fill=1.0, base=0,
                                     pattern=[[-2, CA], [-1, 2], [0, 64]], channel_multiplier=1))
            chain(pool.memset(Y[:, :, 0:TAPS - 1], 0.0))
            pool.memset(ONE[:, :], 1.0).then_inc(const_ready, 1)
            for b in range(2):
                pool.sem_inc(ev[b], 1)
            pool.wait_ge(ld_ws, 16)
            pool.affine_select(out=WS[:, :, :], in_=WS[:, :, :], compare_op=ALU.is_ge, fill=0.0, base=0,
                               pattern=[[0, HA], [1, P]], channel_multiplier=-1).then_inc(const_ready, 1)
            pool_rsqrt(nj["n1"])
            pool.wait_ge(j1["msv"], 1)
            pool.tensor_tensor(STAT[:, 12:16], STAT[:, 8:12], NHALF[:, :], ALU.pow).then_inc(j1["rsv"], 1)
            pool_rsqrt(nj["na"])
            pool_rsqrt(nj["nb"])
            pool_rsqrt(nj["n2"])
            pool_rsqrt(nj["nf"])
            chain(pool.memset(W1B[:, :, :, :], 0.0))
            chain(pool.memset(W2B[:, :, :], 0.0))
            for h in range(2):
                q = slice(64 * h, 64 * h + 64)
                pool.dma_start(W1B[q, :, :, 64 * h:64 * h + 64], w1).then_inc(ld_att, 16)
                pool.dma_start(W2B[q, :, 64 * h:64 * h + 64], w2).then_inc(ld_att, 16)
                pool.dma_start(PEB[q, :, :], pe).then_inc(ld_att, 16)
            pool.dma_start(BF[:, :], bf).then_inc(ld_att, 16)
            chain(pool.iota(DM[:, :], pattern=[[1, S]], base=-(S - P), channel_multiplier=-1,
                            allow_small_or_imprecise_dtypes=True))
            chain(pool.affine_select(out=DM[:, :], in_=DM[:, :], compare_op=ALU.is_ge, fill=NEG, base=S - P,
                                     pattern=[[-1, S]], channel_multiplier=1))
            chain(pool.iota(DC[:, :, :], pattern=[[-P, TC], [16, NCMP]], base=CMPB - 1, channel_multiplier=-1,
                            allow_small_or_imprecise_dtypes=True))
            chain(pool.affine_select(out=DC[:, :, :], in_=DC[:, :, :], compare_op=ALU.is_ge, fill=NEG,
                                     base=-(CMPB - 1), pattern=[[P, TC], [-16, NCMP]], channel_multiplier=1))
            chain(pool.memset(CM[:, :, :], 1.0))
            chain(pool.affine_select(out=CM[:, :, :], in_=CM[:, :, :], compare_op=ALU.is_ge, fill=0.0,
                                     base=-(CMPB - 1), pattern=[[P, TC], [-16, NCMP]], channel_multiplier=1))
            chain(pool.memset(GTS[:, :, :, :], 1.0))
            for h in range(NH):
                chain(pool.memset(SL[:, h:h + 1], 2.0 ** -(h + 1)))
            pool.nop().then_inc(const_ready, 1) if False else pool.memset(STAT[:, 15:16], 0.0).then_inc(const_ready, 1)
            pool_rsqrt(nj["q0"])
            with pool.Fori(0, 4) as it:
                for half in range(2):
                    for i in range(TC):
                        pool.wait_ge(a6["fb"], 8 * it + 4 * half + i + 1)
                        pool.sem_inc(wait_held, 1)
                        dst = FB[:, half, foff(i) + i * P:foff(i) + (i + 1) * P]
                        pool.affine_select(out=dst, in_=dst, compare_op=ALU.is_ge, fill=NEG, base=0,
                                           pattern=[[-1, P]], channel_multiplier=1).then_inc(a6["fbm"], 1)
            for r, q in (("r1", "q1"), ("r2", "q2")):
                pool_rsqrt(nj[r])
                if q == "q2":
                    for w in range(4):
                        chain(pool.iota(PINV[:, w, :], pattern=[[1, S]], base=1, channel_multiplier=0,
                                        allow_small_or_imprecise_dtypes=True))
                    for w in range(4):
                        chain(pool.tensor_scalar(PINV[:, w, :], PINV[:, w, :], float(2 ** (w + 1)), None, ALU.min))
                    pool.memset(PCS[:, :, 0:16], 0.0).then_inc(p10["z"], 1)
                pool_rsqrt(nj[q])
            pool_rsqrt(nj["r3"])
            pool_rsqrt(nj["q3"])
            pool_rsqrt(nj["r4"])

        @blk.tensor
        def _(pe_):
            def ada(s, col, rnd):
                pe_.wait_ge(ld[s], 16 * (rnd + 1))
                for k in range(C):
                    m = pe_.matmul(ADA[:, bass.ds(col, 1)], RAW[s][:, k * P:(k + 1) * P], CACT[:, k:k + 1],
                                   start=(k == 0), stop=(k == C - 1))
                m.then_inc(raw_used, 1)

            pe_.wait_ge(const_ready, 1)
            pe_sum_direct(nj["n1"], C, TMP2)
            pe_.wait_ge(c_ready, 1)
            with pe_.Fori(0, 4) as r:
                for s in range(4):
                    ada(s, 4 * r + s, r)
            pe_bcast(nj["n1"])
            with pe_.Fori(0, 4) as g:
                for t in range(4):
                    pe_.wait_ge(ev[t % 2], 2 * g + t // 2 + 1)
                    block(4 * g + t, t % 2, C, HH, HL, 0, PS[t % 2], True, True, nj["n1"].lo if t == 0 else None)
                    for s in range(1, 4):
                        ada(s, 12 * g + 3 * t + 15 + s, 4 * g + t + 4)
            pe_.wait_ge(ev[0], 7)
            pe_.wait_ge(ev[1], 7)
            for i in range(TC):
                if i >= 2:
                    pe_.wait_ge(j1["vtc"], i - 1)
                for c in range(CA):
                    m = pe_.transpose(PS[2 + i % 2][:, c * P:(c + 1) * P], V[:, c, i * P:(i + 1) * P], IDN[:, :])
                m.then_inc(j1["vt"], 1)
            for c in range(CA):
                pe_.wait_ge(j1["conv"], TAPS * (c + 1))
                if c == 0:
                    pe_.wait_ge(mod_ready, 4)
                if c >= 2:
                    pe_.wait_ge(j1["xc"], c - 1)
                pe_.matmul(PS[4 + c % 2][:, :], GD[:, :], CV[:, c, :], start=True, stop=True).then_inc(j1["gm"], 1)
            for c in range(CA):
                pe_.wait_ge(j1["sq"], c + 1)
                for i in range(TC):
                    m = pe_.matmul(NS[:, 8 * i + 2 * c:8 * i + 2 * c + 2], TMP[:, c % 2, i * P:(i + 1) * P],
                                   GSEL[:, :], start=True, stop=True)
                m.then_inc(j1["var"], 1)
            pe_.wait_ge(const_ready, 2)
            pe_.wait_ge(j1["ln"], TC)
            for c in range(CA):
                if c >= 2:
                    pe_.wait_ge(j1["ya1"], c - 1)
                for i in range(TC):
                    for h in range(2):
                        m = pe_.matmul(PS[2 + c % 2][64 * h:64 * h + 64, i * P:(i + 1) * P],
                                       VT[:, i, (2 * c + h) * 64:(2 * c + h + 1) * 64], WS[:, 2 * c + h, :],
                                       start=True, stop=True)
                m.then_inc(j1["sp"], 1)
            pe_.wait_ge(j1["rc"], 1)
            for i in range(TC):
                m = pe_.transpose(RB[0:GB, i * P:(i + 1) * P], R32[:, 2, 8 * i:8 * i + 8], IDN[:, :])
            m.then_inc(j1["r8t"], 1)
            pe_.wait_ge(j1["r8"], 1)
            for c in range(CA):
                if c >= 2:
                    pe_.wait_ge(j1["gx"], c - 1)
                pe_.matmul(PS[4 + c % 2][:, :], SELG[:, c, :], R8[:, :], start=True, stop=True).then_inc(j1["gb"], 1)
            pe_sum_direct(nj["na"], CA, TMP2)
            pe_bcast(nj["na"])
            pe_sum_direct(nj["nb"], CA, TMP2)
            pe_bcast(nj["nb"])
            with pe_.Fori(0, G["w_out"]) as g:
                for t in range(4):
                    pe_.wait_ge(ev[t % 2], O0["w_out"] // 2 + 2 * g + t // 2)
                    if t == 0:
                        pe_.wait_ge(n_lo, nj["na"].lo + CA)
                        pe_.wait_ge(n_lo, nj["nb"].lo + CA)
                    block(N0["w_out"] + 4 * g + t, t % 2, C, HH, HL, 0, PS[t % 2], True, True)
            pe_sum_acc(nj["n2"], C)
            pe_bcast(nj["n2"])
            pe_phase("ffi0", HH, HL, nj["n2"].lo)
            pe_down("ffo0", ff[0]["hid_lo"])
            pe_sum_acc(nj["nf"], C)
            pe_bcast(nj["nf"])
            pe_sum_direct(nj["q0"], C, TMP2)
            pe_bcast(nj["q0"])

            def lin(name, g, t, ready=None):
                pe_.wait_ge(ev[t % 2], O0[name] // 2 + 2 * g + t // 2)
                block(N0[name] + 4 * g + t, t % 2, C, HH, HL, 0, PS[t % 2], True, True, ready)

            lin("att5", 0, 0, nj["q0"].lo)
            lin("att5", 0, 1)
            lin("att5", 0, 2)
            pe_.wait_ge(a5["cs"], 1)
            for i in range(TC):
                m = pe_.transpose(PS[4][:, i * P:i * P + NH], LF[:, i * P:(i + 1) * P], IDN[0:NH, 0:NH])
            m.then_inc(a5["ct"], 1)
            pe_.wait_ge(ev[1], O0["att5"] // 2 + 1)
            for i in range(TC):
                m = pe_.transpose(PS[5][:, i * P:i * P + 3 * NH], NG[:, i * P:(i + 1) * P], IDN[0:3 * NH, 0:3 * NH])
            m.then_inc(a5["ngt"], 1)
            lin("att5", 0, 3)
            lin("att5", 1, 0)
            lin("att5", 1, 1)
            pe_.wait_ge(ld_att, 16 * 7)
            for kv in range(2):
                pe_.wait_ge(ev[kv], O0["att5"] // 2 + 2)
                for j in range(CMPB):
                    m = pe_.matmul(PS[2 + kv][:, 0:NCMP], W1B[:, kv, j, :], KE[:, kv, :, j], start=(j == 0),
                                   stop=(j == CMPB - 1))
                m.then_inc(a5["hc"], 1)
            for kv in range(2):
                pe_.wait_ge(a5["g1"], kv + 1)
                pe_.matmul(PS[2 + kv][:, 64:64 + NCMP], W2B[:, kv, :], G1[:, kv, :], start=True,
                           stop=True).then_inc(a5["kc2"], 1)

            def v_turn(dst, bank, wait_for, cnt, done, src):
                pe_.wait_ge(wait_for, cnt)
                for i in range(TC):
                    m = pe_.transpose(bank[:, i * P:(i + 1) * P], src[:, i * P:(i + 1) * P], IDN[:, :])
                m.then_inc(done, 1)
            pe_.wait_ge(a5["ctc"], 2)
            v_turn(VST, PS[4], ev[1], O0["att5"] // 2 + 3, a5["vt"], VF)
            lin("att5", 1, 2)
            lin("att5", 1, 3)
            pe_.wait_ge(a5["kcf"], 2)
            pe_.transpose(PS[2][0:NCMP, P:2 * P], KCF[:, 1, :], IDN[:, :]).then_inc(a5["vct"], 1)
            v_turn(VWT, PS[5], ev[1], O0["att5"] // 2 + 4, a5["vt"], VF)

            with pe_.Fori(0, 4) as it:
                for t in range(4):
                    lin("att6", it, t)
                for half in range(2):
                    pe_.wait_ge(a6["csel"], 2 * it + half + 1)
                    pe_.matmul(PS[2 + half][:, :], ONE[0:NH, :], CSEL[:, half, :], start=True,
                               stop=True).then_inc(a6["cb"], 1)
                pe_.wait_ge(ev[0], O0["att6"] // 2 + 2 * it + 2)
                for i in range(TC):
                    m = pe_.transpose(PS[4][:, i * P:(i + 1) * P], VF[:, i * P:(i + 1) * P], IDN[:, :])
                m.then_inc(a6["fvt"], 1)
                pe_.wait_ge(ev[1], O0["att6"] // 2 + 2 * it + 2)
                pe_.wait_ge(a6["fbm"], 8 * it + 8)

                def qk(x):
                    kind, i, half, L = item(x)
                    if x >= 2:
                        pe_.wait_ge(a6["sc"], 32 * it + x - 1)
                    q = slice(64 * half, 64 * half + 64)
                    lhs = (FQ if kind == "fox" else NQ)[q, i * P:(i + 1) * P]
                    rhs = {"fox": FK[q, 0:L], "cmp": KCF[q, 0, :], "slc": KS[q, 0:L], "win": KW[q, 0:L]}[kind]
                    pe_.matmul(PS[2 + x % 2][:, 0:L], lhs, rhs, start=True, stop=True).then_inc(a6["qk"], 1)

                def turn(x):
                    kind, i, half, L = item(x)
                    pe_.wait_ge(a6["nm"], 32 * it + x + 1)
                    if x >= 2:
                        pe_.wait_ge(a6["pt"], 32 * it + x - 1)
                    elif x == 0:
                        pe_.wait_ge(a6["fvc"], it + 1)
                    bank = PS[4 + x % 2]
                    if kind == "cmp":
                        m = pe_.transpose(bank[0:NCMP, 0:P], SC[:, x % 8, 0:NCMP], IDN[:, :])
                    else:
                        for j in range(i + 1):
                            m = pe_.transpose(bank[:, j * P:(j + 1) * P], SC[:, x % 8, j * P:(j + 1) * P], IDN[:, :])
                    m.then_inc(a6["tr"], 1)

                def pv(x):
                    kind, i, half, L = item(x)
                    pe_.wait_ge(a6["pt"], 32 * it + x + 1)
                    q = slice(64 * half, 64 * half + 64)
                    bank = PS[6] if kind == "fox" else PS[7]
                    dst = bank[q, i * P:(i + 1) * P]
                    if kind == "cmp":
                        m = pe_.matmul(dst, VCT[:, q], PT[0:NCMP, x % 3, 0:P], start=True, stop=False,
                                       skip_group_check=True)
                    else:
                        vt = {"fox": FVT, "slc": VST, "win": VWT}[kind]
                        for j in range(i + 1):
                            m = pe_.matmul(dst, vt[:, j, q], PT[:, x % 3, j * P:(j + 1) * P],
                                           start=(kind == "fox" and j == 0),
                                           stop=(kind != "slc" and j == i), skip_group_check=True)
                    m.then_inc(a6["pv"], 1)

                for g in range(9):
                    a, b = 4 * g, 4 * g - 4
                    if g < 8:
                        qk(a)
                        qk(a + 1)
                    if g > 0:
                        turn(b)
                    if g < 8:
                        qk(a + 2)
                    if g > 0:
                        turn(b + 1)
                        pv(b)
                    if g < 8:
                        qk(a + 3)
                    if g > 0:
                        turn(b + 2)
                        pv(b + 1)
                        turn(b + 3)
                        pv(b + 2)
                        pv(b + 3)
            with pe_.Fori(0, G["att_out"]) as g:
                for t in range(4):
                    if t == 0:
                        pe_.wait_ge(a6["ol"], 8)
                    pe_.wait_ge(ev[t % 2], O0["att_out"] // 2 + 2 * g + t // 2)
                    block(N0["att_out"] + 4 * g + t, t % 2, C, AH, AL, 0, PS[t % 2], True, True)
            pe_sum_acc(nj["r1"], C)
            pe_bcast(nj["r1"])
            pe_sum_direct(nj["q1"], C, TMP2)
            pe_bcast(nj["q1"])
            pe_phase("ffi1", HH, HL, nj["q1"].lo)
            pe_down("ffo1", ff[1]["hid_lo"])
            pe_sum_acc(nj["r2"], C)
            pe_bcast(nj["r2"])
            pe_sum_direct(nj["q2"], C, TMP2)
            pe_bcast(nj["q2"])
            for gr in range(4):
                pe_.wait_ge(ld[gr], 16 * (ROUND["pool"] + 1))
                pe_.wait_ge(p10["in"], 2 * gr + 2)
                for mo in range(2):
                    o = 2 * gr + mo
                    pe_.wait_ge(ev[mo], O0["pool"] // 2 + gr)
                    for k in range(2):
                        m = pe_.matmul(PS[mo][:, :], RAW[gr][:, (2 * mo + k) * P:(2 * mo + k + 1) * P],
                                       PIN[:, 2 * gr + k, :], start=(k == 0), stop=(k == 1))
                    if mo == 0:
                        m.then_inc(p10["d"], 1)
                m.then_inc(raw_used, 1)
            pe_sum_acc(nj["r3"], C)
            pe_bcast(nj["r3"])
            pe_sum_direct(nj["q3"], C, TMP2)
            pe_bcast(nj["q3"])
            pe_phase("ffi2", HH, HL, nj["q3"].lo)
            pe_down("ffo2", ff[2]["hid_lo"])
            pe_sum_acc(nj["r4"], C)
            pe_bcast(nj["r4"])

        @blk.scalar
        def _(act):
            act.wait_ge(ld_vec, 16)
            act.activation(CACT[:, :], VEC[:, COL["c"]:COL["c"] + C], ACT.Silu).then_inc(c_ready, 1)
            act.wait_ge(ld_x, 16)
            act_squares(nj["n1"], C, lambda k: X[:, k, :], lambda k: None, TMP2)
            split_hi(0, 0, 0, C, R_P1, first=True)
            act_parts(nj["n1"], C, shift=lambda k: MOD[:, k:k + 1])
            split_hi(1, 1, 0, C, R_P1 + 1, first=True)
            for n in range(16):
                if n < 14:
                    split_hi(n + 2, n % 2, 0, C, R_P1 + n + 2)
                else:
                    split_hi(n + 2, n % 2, n - 14, C, ROUND["w_out"])
                act.wait_ge(mm, n + 1)
                b, c = n % 2, n // 2
                if n < 8:
                    if n % 2:
                        if c >= 1:
                            act.wait_ge(ev[0], c + 1)
                        act.activation(SIG[:, :], PS[1][:, :], ACT.Sigmoid, bias=vcol("b_in", n)).then_inc(ev[1], 1)
                elif n < 12:
                    act.activation(V[:, n - 8, :], PS[b][:, :], ACT.Gelu, bias=vcol("b_in", n)).then_inc(ev[b], 1)
                else:
                    act.activation(U[:, n - 12, :], PS[b][:, :], ACT.Gelu, bias=vcol("b_in", n)).then_inc(ev[b], 1)
            for i in range(TC):
                act.wait_ge(j1["vt"], i + 1)
                act.activation(VT[:, i, :], PS[2 + i % 2][:, :], ACT.Copy).then_inc(j1["vtc"], 1)
            for c in range(CA):
                act.wait_ge(j1["xc"], c + 1)
                if c >= 2:
                    act.wait_ge(j1["var"], c - 1)
                act.activation(TMP[:, c % 2, :], CV[:, c, :], ACT.Square).then_inc(j1["sq"], 1)
            act.wait_ge(j1["v32"], 1)
            act.activation(R32[:, 1, :], R32[:, 0, :], ACT.Sqrt).then_inc(j1["sd"], 1)
            act.wait_ge(j1["r8t"], 1)
            act.activation(R8[:, :], RB[0:GB, :], ACT.Copy).then_inc(j1["r8"], 1)
            act_squares(nj["na"], CA, lambda k: YA[:, k, :], lambda k: act.wait_ge(j1["ya"], k + 1), TMP2)
            act_parts(nj["na"], CA)
            for c in range(CA):
                act.wait_ge(j1["gx"], c + 1)
                act.activation(CV[:, c, :], CV[:, c, :], ACT.Silu, bias=vcol("gn_b", c),
                               scale=vcol("gn_g", c)).then_inc(j1["yb"], 1)
            act_squares(nj["nb"], CA, lambda k: CV[:, k, :], lambda k: act.wait_ge(j1["yb"], k + 1), TMP2)
            act_parts(nj["nb"], CA, k0=CA)
            phase_splits("w_out", act, act_step,
                         lambda g, t: act_gated(nj["n2"], "w_out", 4 * g + t, t % 2, 2 * g + t // 2))
            act_parts(nj["n2"], C, shift=lambda k: MOD[:, 24 + k:25 + k])
            phase_splits("ffi0", act, act_step, lambda g, t: act_ffi("ffi0", ff[0], g, t))
            phase_splits("ffo0", act, act_step,
                         lambda g, t: act_gated(nj["nf"], "ffo0", 2 * g + t // 2, t // 2, g) if t % 2 else None)
            act_squares(nj["q0"], C, lambda k: X[:, k, :], lambda k: act.wait_ge(xs[0], k + 1), TMP2)
            act_parts(nj["q0"], C)

            def evac5(g, t):
                act.wait_ge(mm, N0["att5"] + 4 * g + t + 1)
                bank, b = PS[t % 2], t % 2
                if (g, t) == (0, 0):
                    act.wait_ge(ld_att, 16 * 7)
                    act.activation(LX, bank[0:NH, :], ACT.Identity, bias=BF[:, 0:1]).then_inc(ev[b], 1)
                    act.wait_ge(a5["abs"], 1)
                    act.activation(LE, LA, ACT.Exp, scale=-1.0).then_inc(a5["ex"], 1)
                    act.wait_ge(a5["ex"], 1)
                    act.activation(LA, LE, ACT.Ln, bias=1.0).then_inc(a5["lnx"], 1)
                elif (g, t) == (0, 1):
                    act.activation(NG, bank[0:3 * NH, :], ACT.Sigmoid).then_inc(ev[b], 1)
                elif (g, t) == (1, 0):
                    act.activation(KS[:, :], bank[:, :], ACT.Copy).then_inc(ev[b], 1)
                elif (g, t) == (1, 1):
                    act.activation(VF[:, :], bank[:, :], ACT.Copy).then_inc(ev[b], 1)
                    for kv in range(2):
                        act.wait_ge(a5["hc"], kv + 1)
                        act.activation(G1[:, kv, :], PS[2 + kv][:, 0:NCMP], ACT.Gelu_apprx_tanh).then_inc(a5["g1"], 1)
                    for kv in range(2):
                        act.wait_ge(a5["kc2"], kv + 1)
                        act.activation(KCF[:, kv, :], PS[2 + kv][:, 64:64 + NCMP], ACT.Copy).then_inc(a5["kcf"], 1)
                    act.wait_ge(a5["vt"], 1)
                    act.activation(VST[:, :, :], PS[4][:, :].rearrange("p (a b) -> p a b", a=TC), ACT.Copy).then_inc(a5["vtc"], 1)
                elif (g, t) == (1, 2):
                    act.activation(KW[:, :], bank[:, :], ACT.Copy).then_inc(ev[b], 1)
                elif (g, t) == (1, 3):
                    act.activation(VF[:, :], bank[:, :], ACT.Copy).then_inc(ev[b], 1)
                    act.wait_ge(a5["vct"], 1)
                    act.activation(VCT[:, :], PS[2][0:NCMP, P:2 * P], ACT.Copy).then_inc(a5["vctc"], 1)
                    act.wait_ge(a5["vt"], 2)
                    act.activation(VWT[:, :, :], PS[5][:, :].rearrange("p (a b) -> p a b", a=TC), ACT.Copy).then_inc(a5["vtc"], 1)
            for g in range(2):
                for t in range(4):
                    split_hi(N0["att5"] + 4 * g + t + 2, t % 2, (t + 2) % 4, C, ROUND["att5"] + g + (t >= 2))
                    evac5(g, t)

            def heads(it):
                for half in range(2):
                    act.wait_ge(a6["cb"], 2 * it + half + 1)
                    for i in range(TC):
                        act.activation(FB[:, half, foff(i):foff(i) + (i + 1) * P], PS[2 + half][:, 0:(i + 1) * P],
                                       ACT.Identity, bias=CTS[:, i, half:half + 1], scale=-1.0).then_inc(a6["fb"], 1)
                act.wait_ge(a6["fvt"], it + 1)
                act.activation(FVT[:, :, :], PS[4][:, :].rearrange("p (a b) -> p a b", a=TC), ACT.Copy).then_inc(a6["fvc"], 1)

                def exp(x):
                    kind, i, half, L = item(x)
                    act.wait_ge(a6["sc"], 32 * it + x + 1)
                    if kind == "cmp":
                        act.activation(SC[:, x % 8, 0:L], SC[:, x % 8, 0:L], ACT.Exp, scale=-1.0,
                                       bias=AST[:, 0, x:x + 1]).then_inc(a6["ex"], 1)
                    else:
                        act.activation(SC[:, x % 8, 0:L], SC[:, x % 8, 0:L], ACT.Exp, scale=-1.0,
                                       bias=AST[:, 0, x:x + 1], accum_out=AST[:, 1, x:x + 1]).then_inc(a6["ex"], 1)

                def take(x):
                    kind, i, half, L = item(x)
                    act.wait_ge(a6["tr"], 32 * it + x + 1)
                    if x >= 3:
                        act.wait_ge(a6["pv"], 32 * it + x - 2)
                    if kind == "cmp":
                        act.activation(PT[0:NCMP, x % 3, 0:P], PS[4 + x % 2][0:NCMP, 0:P], ACT.Copy).then_inc(a6["pt"], 1)
                    else:
                        act.activation(PT[:, x % 3, 0:L], PS[4 + x % 2][:, 0:L], ACT.Copy).then_inc(a6["pt"], 1)
                for g in range(9):
                    for j in range(4):
                        if g < 8:
                            exp(4 * g + j)
                        if g > 0:
                            take(4 * g - 4 + j)
                act.wait_ge(a6["pv"], 32 * it + 32)
                act.activation(AH[:, bass.ds(it, 1), :], PS[6][:, :].rearrange("p (a s) -> p a s", a=1),
                               ACT.Copy).then_inc(a6["oh"], 1)
                act.activation(AH[:, bass.ds(it + 4, 1), :], PS[7][:, :].rearrange("p (a s) -> p a s", a=1),
                               ACT.Copy).then_inc(a6["oh"], 1)

            def evac6(g, t):
                act.wait_ge(mm, N0["att6"] + 4 * g + t + 1)
                bank, b = PS[t % 2], t % 2
                dst = (FQ, FK, VF, NQ)[t]
                act.activation(dst[:, :], bank[:, :], ACT.Copy, scale=(1.0, 0.125)[t in (0, 3)]).then_inc(ev[b], 1)
                if t == 3:
                    heads(g)
            phase_splits("att6", act, act_step, evac6)

            def m_phase(name, r, norm_col):
                if name.startswith("ffo"):
                    phase_splits(name, act, act_step, lambda g, t: act_m(
                        nj[r], name, 2 * g + t // 2, t // 2, N0[name] + 4 * g + t + 1,
                        VEC[:, bass.ds(COL["norm_g2"] + norm_col + 2 * g + t // 2, 1)]) if t % 2 else None)
                else:
                    phase_splits(name, act, act_step, lambda g, t: act_m(
                        nj[r], name, 4 * g + t, t % 2, N0[name] + 4 * g + t + 1,
                        VEC[:, bass.ds(COL["norm_g2"] + norm_col + 4 * g + t, 1)]))

            m_phase("att_out", "r1", 8)
            act_squares(nj["q1"], C, lambda k: X[:, k, :], lambda k: act.wait_ge(xs[1], k + 1), TMP2)
            act_parts(nj["q1"], C)
            phase_splits("ffi1", act, act_step, lambda g, t: act_ffi("ffi1", ff[1], g, t))
            m_phase("ffo1", "r2", 24)
            act_squares(nj["q2"], C, lambda k: X[:, k, :], lambda k: act.wait_ge(xs[2], k + 1), TMP2)
            for o in range(C):
                gr, mo = divmod(o, 2)
                if mo == 0:
                    act.wait_ge(p10["d"], gr + 1)
                else:
                    act.wait_ge(raw_used, 64 + gr + 1)
                act.activation(M[:, o, :], PS[mo][:, :], ACT.Copy, scale=PG[:, o:o + 1])
                act.wait_ge(n_acc, nj["r3"].acc + o)
                act.activation(TMP[:, mo, :], PS[mo][:, :], ACT.Square, scale=vcol("pool_s", o)).then_inc(ev[mo], 1)
            split_hi(N0["ffi2"], 0, 0, C, ROUND["ffi2"])
            split_hi(N0["ffi2"] + 1, 1, 1, C, ROUND["ffi2"])
            act_squares(nj["q3"], C, lambda k: X[:, k, :], lambda k: act.wait_ge(xs[3], k + 1), TMP2)
            act_parts(nj["q3"], C)
            phase_splits("ffi2", act, act_step, lambda g, t: act_ffi("ffi2", ff[2], g, t))
            m_phase("ffo2", "r4", 56)

        @blk.vector
        def _(dve):
            dve.wait_ge(const_ready, 1)
            dve_diag(nj["n1"], C, D)
            dve.wait_ge(ld_vec, 16)
            dve.wait_ge(raw_used, 16)
            dve.tensor_tensor(MOD[:, 0:16], ADA[:, 0:16], VEC[:, COL["ada_b"]:COL["ada_b"] + 16], ALU.add).then_inc(mod_ready, 1)
            dve.wait_ge(mod_ready, 1)

            def gain(slot, scale0, norm):
                return dve.scalar_tensor_tensor(GS[:, slot, :], MOD[:, scale0:scale0 + C], 1.0,
                                                VEC[:, COL[norm]:COL[norm] + C], ALU.add, ALU.mult)
            gain(0, 8, "norm1").then_inc(mod_ready, 1)
            dve.wait_ge(mod_ready, 2)
            dve_parts(nj["n1"], C, lambda k: X[:, k, :], lambda k: GS[:, 0, k:k + 1], shift=lambda k: MOD[:, k:k + 1])
            split_lo(0, 0, 0, C)
            split_lo(1, 1, 0, C)
            taps = [(c, k) for c in range(CA) for k in range(TAPS)]
            done = [0]

            def tap():
                c, k = taps[done[0]]
                w = VEC[:, COL["conv_w"] + TAPS * c + k:COL["conv_w"] + TAPS * c + k + 1]
                if k == 0:
                    ins = dve.tensor_scalar(CV[:, c, :], Y[:, c, 0:S], w, vcol("conv_b", c), ALU.mult, ALU.add)
                else:
                    dve.wait_ge(j1["conv"], done[0])
                    ins = dve.scalar_tensor_tensor(CV[:, c, :], Y[:, c, k:k + S], w, CV[:, c, :], ALU.mult, ALU.add)
                ins.then_inc(j1["conv"], 1)
                done[0] += 1

            for n in range(16):
                if n < 14:
                    split_lo(n + 2, n % 2, 0, C)
                else:
                    split_lo(n + 2, n % 2, n - 14, C)
                if n < 8 and n % 2:
                    c = n // 2
                    dve.wait_ge(ev[1], c + 2)
                    dve.wait_ge(mm, n)
                    dve.scalar_tensor_tensor(Y[:, c, TAPS - 1:], PS[0][:, :], vcol("b_in", n - 1), SIG[:, :],
                                             ALU.add, ALU.mult).then_inc(ev[0], 1)
                    dve.wait_ge(ev[0], c + 2)
                if n >= 1:
                    for _ in range(9 if n > 1 else 6):
                        if done[0] < len(taps) and (n >= 7 or taps[done[0]][0] <= (n - 1) // 2):
                            tap()
            while done[0] < len(taps):
                tap()
            dve.wait_ge(raw_used, 64)
            dve.tensor_tensor(MOD[:, 16:64], ADA[:, 16:64], VEC[:, COL["ada_b"] + 16:COL["ada_b"] + 64], ALU.add).then_inc(mod_ready, 1)
            dve.tensor_tensor(PG[:, :], VEC[:, COL["pool_s"]:COL["pool_s"] + C],
                              VEC[:, COL["norm_g2"] + 40:COL["norm_g2"] + 48], ALU.mult).then_inc(mod_ready, 1)
            dve.wait_ge(mod_ready, 3)
            gain(1, 32, "norm2").then_inc(mod_ready, 1)
            gain(2, 56, "normf").then_inc(mod_ready, 1)
            for i in range(TC):
                dve.wait_ge(j1["vtc"], i + 1)
                dve.bn_stats(BN[:, i, :], VT[:, i, :]).then_inc(j1["bn"], 1)
            for i in range(TC):
                dve.wait_ge(j1["bn"], i + 1)
                dve.bn_aggr(MV[:, i, :], BN[:, i, :]).then_inc(j1["bna"], 1)
            dve.wait_ge(j1["bna"], TC)
            dve.tensor_scalar(STAT[:, 8:12], MV[:, :, 1], EPS, None, ALU.add).then_inc(j1["msv"], 1)
            for c in range(CA):
                dve.wait_ge(j1["gm"], c + 1)
                dve.tensor_tensor(CV[:, c, :], CV[:, c, :], PS[4 + c % 2][:, :], ALU.subtract).then_inc(j1["xc"], 1)
            dve.wait_ge(ld_ln, 16)
            dve.wait_ge(j1["rsv"], 1)
            for i in range(TC):
                dve.scalar_tensor_tensor(VT[:, i, :], VT[:, i, :], MV[:, i, 0:1], LNR[:, 0, :], ALU.subtract,
                                         ALU.mult).then_inc(j1["ln1"], 1)
            for i in range(TC):
                dve.wait_ge(j1["ln1"], i + 1)
                dve.scalar_tensor_tensor(VT[:, i, :], VT[:, i, :], STAT[:, 12 + i:13 + i], LNR[:, 1, :], ALU.mult,
                                         ALU.add).then_inc(j1["ln"], 1)
            dve.wait_ge(j1["var"], CA)
            dve.tensor_scalar(R32[:, 0, :], NS[:, 0:32], EPS, None, ALU.add).then_inc(j1["v32"], 1)
            dve.wait_ge(j1["sd"], 1)
            dve.reciprocal(R32[:, 2, :], R32[:, 1, :]).then_inc(j1["rc"], 1)
            dve.wait_ge(ld_bs, 16 * HA)
            dve.wait_ge(ev[0], 9)
            dve.wait_ge(ev[1], 9)
            for c in range(CA):
                dve.wait_ge(j1["sp"], c + 1)
                dve.tensor_tensor(YA[:, c, :].rearrange("p (i t) -> p i t", i=TC),
                                  PS[2 + c % 2][:, :].rearrange("p (i t) -> p i t", i=TC),
                                  BS[:, c:c + 1, :].to_broadcast([P, TC, P]), ALU.add).then_inc(j1["ya1"], 1)
                dve.wait_ge(j1["ya1"], c + 1)
                dve.tensor_tensor(YA[:, c, :], YA[:, c, :], U[:, c, :], ALU.mult).then_inc(j1["ya"], 1)
            for c in range(CA):
                dve.wait_ge(j1["gb"], c + 1)
                dve.tensor_tensor(CV[:, c, :], CV[:, c, :], PS[4 + c % 2][:, :], ALU.mult).then_inc(j1["gx"], 1)
            dve_diag(nj["na"], CA, DA)
            dve_parts(nj["na"], CA, lambda k: YA[:, k, :], lambda k: vcol("on_a", k))
            dve_diag(nj["nb"], CA, DA)
            dve_parts(nj["nb"], CA, lambda k: CV[:, k, :], lambda k: vcol("on_b", k), k0=CA)
            dve_clear_acc(nj["n2"])
            dve.wait_ge(mod_ready, 6)
            phase_splits("w_out", dve, dve_step, lambda g, t: dve_gated(
                nj["n2"], "w_out", (4 * g + t, N0["w_out"] + 4 * g + t + 1), t % 2, 16))
            dve_diag(nj["n2"], 1, D)
            dve_parts(nj["n2"], C, lambda k: X[:, k, :], lambda k: GS[:, 1, k:k + 1],
                      shift=lambda k: MOD[:, 24 + k:25 + k])
            phase_splits("ffi0", dve, dve_step, lambda g, t: dve_ffi("ffi0", ff[0], g, t))
            dve.wait_ge(ff[0]["hid_lo"], CF)
            dve_clear_acc(nj["nf"])
            phase_splits("ffo0", dve, dve_step, lambda g, t: dve_gated(
                nj["nf"], "ffo0", (2 * g + t // 2, N0["ffo0"] + 4 * g + t + 1), t // 2, 40) if t % 2 else None)
            dve_diag(nj["nf"], 1, D)
            dve.wait_ge(n_rb, nj["nf"].count)
            for k in range(C):
                if k >= 2:
                    dve.wait_ge(xs[0], k - 1)
                dve.scalar_tensor_tensor(TMP[:, k % 2, :], X[:, k, :], GS[:, 2, k:k + 1], RB[:, :], ALU.mult,
                                         ALU.mult).then_inc(n_t, 1)
                dve.wait_ge(n_t, nj["nf"].t + k + 1)
                dve.tensor_scalar(X[:, k, :], TMP[:, k % 2, :], MOD[:, 48 + k:49 + k], None, ALU.add).then_inc(xs[0], 1)
            dve_diag(nj["q0"], C, D)
            dve.wait_ge(xs[0], C)
            dve_parts(nj["q0"], C, lambda k: X[:, k, :], lambda k: vcol("norm_g2", k))

            def evac5(g, t):
                done_n = N0["att5"] + 4 * g + t + 1
                if (g, t) == (0, 0):
                    dve.wait_ge(ev[0], O0["att5"] // 2 + 1)
                    dve.scalar_tensor_tensor(LA, LX, -1.0, LX, ALU.mult, ALU.max).then_inc(a5["abs"], 1)
                    dve.memset(LF[:, :], 1.0).then_inc(a5["lf"], 1)
                    dve.wait_ge(a5["lnx"], 1)
                    dve.scalar_tensor_tensor(LE, LX, 0.0, LA, ALU.min, ALU.subtract).then_inc(a5["lf"], 1)
                    dve.wait_ge(a5["lf"], 2)
                    dve.tensor_tensor_scan(LF[:, :], ONES_ROW, LE, 0.0, ALU.mult, ALU.add).then_inc(a5["cs"], 1)
                elif t in (2, 3) and g == 0:
                    kv = t - 2
                    dve.wait_ge(mm, done_n)
                    dve.wait_ge(ld_att, 16 * 7)
                    src = PS[t % 2][:, :].rearrange("p (n j) -> p n j", j=16)
                    pe_v = PEB[:, kv:kv + 1, :]
                    dve.tensor_tensor(KE[:, kv, :, 0:16], src[:, 0:NCMP, :], pe_v[:, :, 0:16].to_broadcast([P, NCMP, 16]),
                                      ALU.add)
                    dve.tensor_tensor(KE[:, kv, :, 16:32], src[:, 1:NCMP + 1, :],
                                      pe_v[:, :, 16:32].to_broadcast([P, NCMP, 16]), ALU.add).then_inc(ev[t % 2], 1)
                    if kv == 0:
                        dve.wait_ge(a5["ct"], 1)
                        dve.tensor_copy(CTK[:, :, :], PS[4][:, :].rearrange("p (i t) -> p i t", i=TC)[:, :, 0:NH]).then_inc(a5["ctc"], 1)
                        dve.wait_ge(a5["ngt"], 1)
                        dve.tensor_copy(GT[:, :, :], PS[5][:, :].rearrange("p (i t) -> p i t", i=TC)[:, :, 0:3 * NH]).then_inc(a5["ctc"], 1)
            ONES_ROW = ONE[0:NH, 0:1].to_broadcast([NH, S])
            for g in range(2):
                for t in range(4):
                    split_lo(N0["att5"] + 4 * g + t + 2, t % 2, (t + 2) % 4, C)
                    evac5(g, t)
            dve.wait_ge(a5["ctc"], 2)
            dve.wait_ge(const_ready, 3)
            dve.wait_ge(a5["vtc"], 2)

            def heads(it):
                def score(x):
                    kind, i, half, L = item(x)
                    dve.wait_ge(a6["qk"], 32 * it + x + 1)
                    if x == 0:
                        dve.wait_ge(a6["fbm"], 8 * it + 8)
                    if x >= 8:
                        dve.wait_ge(a6["tr"], 32 * it + x - 7)
                    bias = {"fox": FB[:, half, foff(i):foff(i) + L] if kind == "fox" else None,
                            "cmp": CLB[:, half, i, :]}.get(kind, ALB[:, half, S - L:S])
                    dve.sem_inc(wait_held, 1)
                    dve.tensor_tensor_reduce(SC[:, x % 8, 0:L], PS[2 + x % 2][:, 0:L], bias, -1.0, 3.0e38, ALU.add,
                                             ALU.min, AST[:, 0, x:x + 1]).then_inc(a6["sc"], 1)

                def stats(g):
                    x = 4 * g + 1
                    dve.wait_ge(a6["ex"], 32 * it + x + 1)
                    i = item(x)[1]
                    dve.tensor_tensor_reduce(SC[:, x % 8, 0:NCMP], SC[:, x % 8, 0:NCMP], CM[:, i, :], 1.0, 0.0,
                                             ALU.mult, ALU.add, AST[:, 1, x:x + 1]).then_inc(a6["cm"], 1)
                    dve.wait_ge(a6["ex"], 32 * it + 4 * g + 4)
                    dve.wait_ge(a6["cm"], 8 * it + g + 1)
                    cols = slice(4 * g, 4 * g + 4)
                    dve.tensor_scalar(AST[:, 1, cols], AST[:, 1, cols], 1e-30, None, ALU.max).then_inc(a6["mx"], 1)
                    dve.wait_ge(a6["mx"], 8 * it + g + 1)
                    dve.reciprocal(AST[:, 2, cols], AST[:, 1, cols]).then_inc(a6["rc"], 1)
                    dve.wait_ge(a6["rc"], 8 * it + g + 1)

                def norm(x):
                    kind, i, half, L = item(x)
                    sc = SC[:, x % 8, 0:L]
                    dve.tensor_scalar(sc, sc, AST[:, 2, x:x + 1], GTS[:, i, half, x % 4:x % 4 + 1], ALU.mult,
                                      ALU.mult).then_inc(a6["nm"], 1)
                for g in range(9):
                    for j in range(4):
                        if g < 8:
                            score(4 * g + j)
                        if g > 0:
                            if j == 0:
                                stats(g - 1)
                            norm(4 * g - 4 + j)
                for b in range(2):
                    dve.wait_ge(a6["oh"], 2 * it + b + 1)
                    dve.tensor_tensor(AL[:, bass.ds(it + 4 * b, 1), :], PS[6 + b][:, :].rearrange("p (a s) -> p a s", a=1),
                                      AH[:, bass.ds(it + 4 * b, 1), :].bitcast(F32), ALU.subtract).then_inc(a6["ol"], 1)

            def evac6(g, t):
                if t == 0:
                    for half in range(2):
                        h = 2 * g + half
                        dve.tensor_scalar(CSEL[:, half, :], LF[:, :], IDN[0:NH, bass.ds(h, 1)], None, ALU.mult).then_inc(a6["csel"], 1)
                    dve.tensor_copy(CTS[:, :, :], CTK[:, :, bass.ds(2 * g, 2)]).then_inc(a6["stg"], 1)
                    for half in range(2):
                        h = g + 4 * half
                        dve.tensor_copy(GTS[:, :, half, 1:4], GT[:, :, bass.ds(3 * h, 3)]).then_inc(a6["stg"], 1)
                        dve.tensor_scalar(ALB[:, half, :], DM[:, :], SL[:, bass.ds(h, 1)], None, ALU.mult).then_inc(a6["stg"], 1)
                        dve.tensor_scalar(CLB[:, half, :, :], DC[:, :, :], SL[:, bass.ds(h, 1)], None, ALU.mult).then_inc(a6["stg"], 1)
                    dve.wait_ge(a6["stg"], 7 * g + 7)
                if t == 3:
                    heads(g)
            phase_splits("att6", dve, dve_step, evac6)

            def m_phase(name, r):
                dve_clear_acc(nj[r])
                if name.startswith("ffo"):
                    phase_splits(name, dve, dve_step, lambda g, t: dve_m(nj[r], name, 2 * g + t // 2, t // 2, g) if t % 2 else None)
                else:
                    phase_splits(name, dve, dve_step, lambda g, t: dve_m(nj[r], name, 4 * g + t, t % 2, 2 * g + t // 2))

            m_phase("att_out", "r1")
            dve_diag(nj["r1"], 1, D)
            dve_add_normed(nj["r1"], xs[1])
            dve_diag(nj["q1"], C, D)
            dve.wait_ge(xs[1], C)
            dve_parts(nj["q1"], C, lambda k: X[:, k, :], lambda k: vcol("norm_g2", 16 + k))
            phase_splits("ffi1", dve, dve_step, lambda g, t: dve_ffi("ffi1", ff[1], g, t))
            dve.wait_ge(ff[1]["hid_lo"], CF)
            m_phase("ffo1", "r2")
            dve_diag(nj["r2"], 1, D)
            dve_add_normed(nj["r2"], xs[2])
            dve_diag(nj["q2"], C, D)
            dve.wait_ge(xs[2], C)
            dve.wait_ge(n_rb, nj["q2"].count)
            dve.wait_ge(p10["z"], 1)
            dve.reciprocal(PINV[:, :, 0:16], PINV[:, :, 0:16]).then_inc(p10["inv"], 1)
            for w in range(4):
                dve.memset(PINV[:, w, 16:S], 0.5 ** (w + 1)).then_inc(p10["inv"], 1)
            for k in range(C):
                dve.scalar_tensor_tensor(PUT[:, k, :], X[:, k, :], vcol("norm_g2", 32 + k), RB[:, :], ALU.mult,
                                         ALU.mult).then_inc(p10["u"], 1)
            for k in range(C):
                w = 2 ** (k // 2 + 1)
                dve.wait_ge(p10["u"], k + 1)
                if k >= 2:
                    dve.wait_ge(p10["in"], k - 1)
                dve.tensor_tensor_scan(PCS[:, k % 2, 16:], ONE[:, 0:1].to_broadcast([P, S]), PUT[:, k, :], 0.0,
                                       ALU.mult, ALU.add).then_inc(p10["cs"], 1)
                dve.wait_ge(p10["cs"], k + 1)
                dve.tensor_tensor(PTM[:, k % 2, :], PCS[:, k % 2, 16:], PCS[:, k % 2, 16 - w:16 - w + S], ALU.subtract).then_inc(p10["e"], 1)
                dve.wait_ge(p10["e"], 2 * k + 1)
                if k == 0:
                    dve.wait_ge(p10["inv"], 5)
                dve.tensor_tensor(PTM[:, k % 2, :], PTM[:, k % 2, :], PINV[:, k // 2, :], ALU.mult).then_inc(p10["e"], 1)
                dve.wait_ge(p10["e"], 2 * k + 2)
                dve.tensor_tensor(PIN[:, k, :], PTM[:, k % 2, :], PUT[:, k, :], ALU.subtract).then_inc(p10["in"], 1)
            dve_clear_acc(nj["r3"])
            for o in range(C):
                dve_m(nj["r3"], "pool", o, o % 2, o // 2)
            split_lo(N0["ffi2"], 0, 0, C)
            split_lo(N0["ffi2"] + 1, 1, 1, C)
            dve_diag(nj["r3"], 1, D)
            dve_add_normed(nj["r3"], xs[3])
            dve_diag(nj["q3"], C, D)
            dve.wait_ge(xs[3], C)
            dve_parts(nj["q3"], C, lambda k: X[:, k, :], lambda k: vcol("norm_g2", 48 + k))
            phase_splits("ffi2", dve, dve_step, lambda g, t: dve_ffi("ffi2", ff[2], g, t))
            dve.wait_ge(ff[2]["hid_lo"], CF)
            m_phase("ffo2", "r4")
            dve_diag(nj["r4"], 1, D)
            dve_add_normed(nj["r4"], xs[4])


def _blocks(w):
    k, m = w.shape
    return w.reshape(k // P, P, m // P, P).transpose(2, 1, 0, 3).reshape(m // P, P, k)


def _down(w):
    return w.reshape(2, KH, P, C, P).transpose(3, 0, 2, 1, 4).reshape(2 * C, P, KH * P)


def _cols(v):
    return v.reshape(-1, P).T


def _layout(a):
    w = a["w_in"][0]
    u, v, val, gate = (_blocks(w[:, i * DA:(i + 1) * DA]) for i in range(4))
    order = [x for c in range(CA) for x in (val[c:c + 1], gate[c:c + 1])] + [v, u]
    b = _cols(a["b_in"][0])
    bu, bv, bval, bgate = (b[:, 4 * i:4 * i + 4] for i in range(4))
    b_cols = [x for c in range(CA) for x in (bval[:, c:c + 1], bgate[:, c:c + 1])] + [bv, bu]
    conv = a["b_conv_w"][0].T.reshape(CA, P, TAPS).transpose(1, 0, 2).reshape(P, CA * TAPS)
    vec = np.concatenate([
        _cols(a["c"][0]), _cols(a["ada_b"][0]), _cols(a["ada_f_b"]), _cols(a["norm1_g"][0]), _cols(a["norm2_g"][0]),
        _cols(a["norm_f_g"]), *b_cols, _cols(a["b_gn_g"][0]), _cols(a["b_gn_b"][0]), _cols(a["b_conv_b"][0]), conv,
        _cols(a["out_norm_a_g"][0]), _cols(a["out_norm_b_g"][0]), _cols(a["norm_g_2"].reshape(-1)),
        _cols(a["pool_scale_2"][0])], axis=1)
    f = _blocks(a["w_ffn_in"][0])
    gu = lambda g_, u_: np.stack([g_, u_], axis=1).reshape(2 * CF, P, D)
    t = a["attn_w_in_2"][0]
    fq, fk, fv = (t[:, 512 * i:512 * (i + 1)] for i in range(3))
    ffw, nq, rest, ng = t[:, 1536:1544], t[:, 1544:2056], t[:, 2056:2824], t[:, 2824:2848]
    pad = lambda m: np.concatenate([m, np.zeros((D, P - m.shape[1]), m.dtype)], axis=1)
    pair = lambda m: m.reshape(m.shape[0], 2, 4, DH).transpose(0, 2, 1, 3).reshape(m.shape[0], 512)
    nqb, fqb, fkb, fvb = _blocks(pair(nq)), _blocks(fq), _blocks(fk), _blocks(fv)
    att = np.concatenate([_blocks(pad(ffw)), _blocks(pad(ng)), _blocks(rest)] +
                         [x[c:c + 1] for c in range(4) for x in (fqb, fkb, fvb, nqb)])
    ow = a["attn_w_out_2"][0]
    ow = np.concatenate([ow[:512], ow[512:].reshape(2, 4, DH, D).transpose(1, 0, 2, 3).reshape(512, D)])
    pw = a["pool_w_2"][0].reshape(4, 2, P, 2, P).transpose(0, 2, 3, 1, 4).reshape(4, P, 4 * P)
    out = {
        "xT": a["x"][0].T.reshape(C, P, S).transpose(1, 0, 2), "vec": vec,
        "ada_w": np.concatenate([_blocks(a["ada_w"][0]), _blocks(a["ada_f_w"])]),
        "w_in": np.concatenate(order), "w_out": _blocks(a["w_out"][0]), "ffi": gu(f[:CF], f[CF:]),
        "ffo": _down(a["w_ffn_out"][0]), "ln_rows": np.stack([a["a_ln_g"][0], a["a_ln_b"][0]]),
        "ws": a["a_spatial_w"][0].transpose(2, 0, 1), "bs": a["a_spatial_b"][0], "att_w": att,
        "att_out": _blocks(ow), "bf": a["fox_b_f_2"][0].reshape(NH, 1), "pe": a["nsa_cmp_pe_2"][0].transpose(2, 0, 1),
        "w1": a["nsa_cmp_w1_2"][0].reshape(2, CMPB, DH, DH).transpose(2, 0, 1, 3),
        "w2": a["nsa_cmp_w2_2"][0].transpose(1, 0, 2), "pool_w": pw,
        "f2i": np.concatenate([gu(_blocks(a["ffn_w_gate_2"][i]), _blocks(a["ffn_w_up_2"][i])) for i in range(2)]),
        "f2o": np.concatenate([_down(a["ffn_w_down_2"][i]) for i in range(2)]),
    }
    return {k: np.ascontiguousarray(v) for k, v in out.items()}


def kernel(**inputs):
    import concourse.bacc as bacc
    from concourse.bass_utils import run_bass_kernel_spmd

    nc = bacc.Bacc("TRN2", target_bir_lowering=False, num_devices=1)
    arrays = {f"in_{k}": v for k, v in _layout({k: np.asarray(v) for k, v in inputs.items()}).items()}
    args = [nc.dram_tensor(k, v.shape, mybir.dt.from_np(v.dtype), kind="ExternalInput").ap()
            for k, v in arrays.items()]
    out = nc.dram_tensor("out_T", (P, C, S), F32, kind="ExternalOutput").ap()
    build_program(nc, *args, out)
    r = run_bass_kernel_spmd(nc, [arrays], core_ids=[0])
    got = r.results[0]["out_T"]
    return np.ascontiguousarray(got.transpose(1, 0, 2).reshape(D, S).T).reshape(1, S, D)
```

```python
from contextlib import ExitStack

import numpy as np

import concourse.bass as bass
from concourse import mybir

F32 = mybir.dt.float32
F32R = mybir.dt.float32r
ALU = mybir.AluOpType
ACT = mybir.ActivationFunctionType

P = 128
S = 512
D = 1024
C = D // P
TC = S // P
DA = D // 2
CA = DA // P
HA = 8
GB = 8
TAPS = 31
FF = 2816
CF = FF // P
KH = CF // 2
NH = 8
DH = 64
NCMP = (S // 16) - 1
CMPB = 32
DVE_TAPS = 8
EPS = 1e-6
NEG = -1e30

_SIZES = [("c", 8), ("ada_b", 64), ("norm1", 8), ("norm2", 8), ("normf", 8), ("b_in", 16), ("gn_g", 4),
          ("gn_b", 4), ("conv_b", 4), ("conv_w", 4 * TAPS), ("on_a", 4), ("on_b", 4), ("norm_g2", 64),
          ("pool_s", 8)]
COL = {}
_at = 0
for _n, _w in _SIZES:
    COL[_n] = _at
    _at += _w
NVEC = _at

ADA_N = 8
ADA_A = 2 * C
ADA_B = (ADA_N - 4) * C
ADA_C = 2 * C
PER = ADA_B // 16
R_P1 = ADA_A // 4
G = {"w_out": 2, "ffi0": 11, "ffo0": 4, "att5": 2, "att6": 4, "att_out": 2, "ffi1": 11, "ffo1": 4,
     "pool": 1, "ffi2": 11, "ffo2": 4}
ROUND, N0, O0 = {}, {}, {}
_r, _b, _o = R_P1 + 4, 16, 2 + 16
for _n in ("w_out", "ffi0", "ffo0", "att5", "att6", "att_out", "ffi1", "ffo1", "pool", "ffi2", "ffo2"):
    ROUND[_n], N0[_n], O0[_n] = _r, _b, _o
    _r += G[_n]
    _b += 0 if _n == "pool" else 4 * G[_n]
    _o += 8 if _n == "pool" else (2 if _n.startswith("ffo") else 4) * G[_n]


def build_program(nc, xT, vec, ada_w, w_in, w_out, ffi, ffo, ln_rows, ws, bs, att_w, att_out, bf, pe, w1, w2,
                  pool_w, f2i, f2o, outT):
    ctx = ExitStack()
    with ctx:
        def sb(name, shape, dt=F32):
            return ctx.enter_context(nc.sbuf_tensor(name, shape, dt))

        def sem(name):
            return ctx.enter_context(nc.semaphore(name))

        RAW = [sb(f"raw{i}", [P, KH * P]) for i in range(4)]
        WH = [sb(f"w_hi{i}", [P, KH * P], F32R) for i in range(2)]
        WL = [sb(f"w_lo{i}", [P, KH * P], F32R) for i in range(2)]
        X = sb("x_res", [P, C, S])
        HH = sb("h_hi", [P, C, S], F32R)
        HL = sb("h_lo", [P, C, S], F32R)
        TMP = sb("tmp", [P, 2, S])
        TMP2 = sb("tmp2", [P, 2, S])
        VEC = sb("vec_sb", [P, NVEC])
        MOD = sb("mod", [P, 64])
        GS = sb("gs", [P, 3, C])
        PG = sb("pool_gs", [P, C])
        CACT = sb("c_act", [P, C])
        IDN = sb("ident", [P, P])
        ONE = sb("ones", [P, P])
        STAT = sb("stat", [P, 16])
        NHALF = sb("nhalf", [P, 4])
        ACC = TMP2[:, 0, :]
        DG = TMP2[:, 1, :]
        LX, LA, LE, NG = TMP[0:NH, 0, :], TMP[0:NH, 1, :], TMP2[0:NH, 0, :], TMP2[0:3 * NH, 1, :]
        PS = [ctx.enter_context(nc.psum_tensor(f"bank{i}", [P, S], F32)) for i in range(8)]
        NS, RB = PS[6], PS[7]

        with ExitStack() as life:
            def lb(name, shape, dt=F32):
                return life.enter_context(nc.sbuf_tensor(name, shape, dt))
            U = lb("u_act", [P, CA, S])
            V = lb("v_act", [P, CA, S])
            Y = lb("y_pad", [P, CA, S + TAPS - 1])
            SIG = lb("sig", [P, S])
            CV = lb("conv", [P, CA, S])
            VT = lb("v_tok", [P, TC, DA])
            LNR = lb("ln_rows_sb", [P, 2, DA])
            WS = lb("ws_sb", [P, HA, P])
            BS = lb("bs_sb", [P, CA, P])
            YA = V
            GD = lb("gd", [P, P])
            GSEL = lb("gsel", [P, 2])
            SELG = lb("selg", [GB, CA, P])
            BN = lb("bn", [P, TC, 6])
            MV = lb("mv", [P, TC, 2])
            R32 = lb("r32", [P, 3, 32])
            AAC = lb("ada_acc", [P, ADA_N - 2, D])
            AWB = lb("ada_w", [P, 4, D])
            R8 = SIG[0:GB, :]
        with ExitStack() as life:
            def lb2(name, shape, dt=F32):
                return life.enter_context(nc.sbuf_tensor(name, shape, dt))
            with ExitStack() as sub:
                W1B = sub.enter_context(nc.sbuf_tensor("w1b", [P, 2, CMPB, P], F32))
            AH = lb2("ao_hi", [P, C, S], F32R)
            AL = lb2("ao_lo", [P, C, S], F32R)
            W2B = lb2("w2b", [P, 2, P])
            PEB = lb2("peb", [P, 2, CMPB])
            BF = lb2("bf_sb", [NH, 1])
            LF = lb2("log_f_sum", [NH, S])
            CTK = lb2("c_tok", [P, TC, NH])
            GT = lb2("g_tok", [P, TC, 3 * NH])
            with ExitStack() as sub:
                KE = sub.enter_context(nc.sbuf_tensor("ke", [P, 2, NCMP, CMPB], F32))
            FB = lb2("fox_bias", [P, 2, 10 * P])
            G1 = lb2("g1", [P, 2, NCMP])
            KCF = lb2("kcf", [P, 2, NCMP])
            VCT = lb2("vct", [NCMP, P])
            KS = lb2("k_slc", [P, S])
            KW = lb2("k_win", [P, S])
            VF = lb2("vf", [P, S])
            VST = lb2("v_slc_tok", [P, TC, P])
            VWT = lb2("v_win_tok", [P, TC, P])
            FQ = lb2("fq", [P, S])
            FK = lb2("fk", [P, S])
            NQ = lb2("nq", [P, S])
            FVT = lb2("fv_tok", [P, TC, P])
            CSEL = lb2("c_sel", [NH, 2, S])
            DM = lb2("dist", [P, S])
            DC = lb2("dist_cmp", [P, TC, NCMP])
            CM = lb2("mask_cmp", [P, TC, NCMP])
            ALB = lb2("alibi", [P, 2, S])
            CLB = lb2("alibi_cmp", [P, 2, TC, NCMP])
            SL = lb2("slopes", [P, NH])
            CTS = lb2("c_tok_it", [P, TC, 2])
            GTS = lb2("g_it", [P, TC, 2, 4])
            SC = lb2("scores", [P, 8, S])
            PT = lb2("p_t", [P, 3, S])
            AST = lb2("att_stat", [P, 3, 32])
        with ExitStack() as life:
            def lb3(name, shape, dt=F32):
                return life.enter_context(nc.sbuf_tensor(name, shape, dt))
            FH = lb3("hid_hi", [P, CF, S], F32R)
            FL = lb3("hid_lo", [P, CF, S], F32R)
            M = lb3("m_out", [P, C, S])
            LW, LACC = (M[:, 4 * i:4 * i + 4, :].rearrange("p (r a) s -> p r (a s)", r=2) for i in range(2))
        with ExitStack() as life:
            PUT = life.enter_context(nc.sbuf_tensor("pool_u", [P, C, S], F32))
            PCS = life.enter_context(nc.sbuf_tensor("pool_cs", [P, 2, S + 16], F32))
            PINV = life.enter_context(nc.sbuf_tensor("pool_inv", [P, 4, 16], F32))
            PIN = life.enter_context(nc.sbuf_tensor("pool_in", [P, C, S], F32))
            PTM = life.enter_context(nc.sbuf_tensor("pool_tmp", [P, 2, S], F32))

        ld = [sem(f"raw_loaded{i}") for i in range(4)]
        whi, wlo, mm = sem("w_hi_ready"), sem("w_lo_ready"), sem("block_multiplied")
        ev = [sem(f"bank{i}_evacuated") for i in range(2)]
        raw_used = sem("raw_block_used")
        ld_ada = [sem(f"ada_block_loaded{i}") for i in range(4)]
        ada_used = sem("ada_block_added")
        ld_late = [sem(f"late_ada_loaded{i}") for i in range(2)]
        late_mul, late_used = sem("late_ada_multiplied"), sem("late_ada_added")
        ada_mul = sem("ada_block_multiplied")
        ada_sum = sem("ada_vector_summed")
        ld_x, ld_vec, ld_ln, ld_ws, ld_bs, ld_att = (sem(n) for n in (
            "x_loaded", "vec_loaded", "ln_loaded", "ws_loaded", "bs_loaded", "att_const_loaded"))
        const_ready, pool_chain, c_ready, mod_ready = (sem(n) for n in (
            "const_ready", "pool_chain", "c_ready", "mod_ready"))
        store_done = sem("store_done")
        ld_small = sem("att_vectors_loaded")
        wait_held = sem("wait_held")
        x_ready = sem("x_final")

        n_ms = sem("norm_mean_square")
        n_rs = sem("norm_power")
        n_dg = sem("norm_diagonal")
        n_rb = sem("norm_broadcast")

        n_sq = sem("norm_squares")
        n_used = sem("norm_squares_summed")
        n_acc = sem("norm_running_sum")
        n_t = sem("normed_chunk")
        n_hi = sem("normed_chunk_hi")
        n_lo = sem("normed_chunk_lo")

        class Norm:
            def __init__(self, count, at, n_acc_):
                self.count = count
                self.sq, self.used, self.acc, self.t, self.hi, self.lo = at
                self.acc_end = at[2] + n_acc_

        kinds = (("n1", C, 1, C - 1, C, C, C), ("na", CA, 1, CA - 1, CA, CA, CA), ("nb", CA, 1, CA - 1, CA, CA, CA),
                 ("n2", C, 1, C + 1, C, C, C), ("nf", C, 1, C + 1, C, 0, 0), ("q0", C, 1, C - 1, C, C, C),
                 ("r1", 0, 1, C + 1, C, 0, 0), ("q1", C, 1, C - 1, C, C, C), ("r2", 0, 1, C + 1, C, 0, 0),
                 ("q2", C, 1, C - 1, 0, 0, 0), ("r3", 0, 1, C + 1, C, 0, 0), ("q3", C, 1, C - 1, C, C, C),
                 ("r4", 0, 1, C + 1, C, 0, 0))
        nj, at = {}, [0] * 6
        for q, (k, *counts) in enumerate(kinds):
            nj[k] = Norm(q + 1, at, counts[2])
            at = [a + b for a, b in zip(at, counts)]

        def split_hi(n, par, s, kc, rnd, first=False):
            nc.scalar.wait_ge(ld[s], 16 * (rnd + 1))
            if not first:
                nc.scalar.wait_ge(mm, n - 1)
            nc.scalar.activation(WH[par][:, 0:kc * P], RAW[s][:, 0:kc * P], ACT.Copy).then_inc(whi, 1)

        def split_lo(n, par, s, kc):
            nc.vector.wait_ge(whi, n + 1)
            nc.vector.tensor_tensor(WL[par][:, 0:kc * P], RAW[s][:, 0:kc * P],
                                    WH[par][:, 0:kc * P].bitcast(F32), ALU.subtract).then_inc(wlo, 1)

        def groups(eng, count, uniform, body):
            n = count if uniform else count - 1
            if n:
                with eng.Fori(0, n) as g:
                    body(g, False)
            if not uniform:
                body(count - 1, True)

        def follow(name):
            return {"w_out": (C, ROUND["ffi0"]), "ffi0": (KH, ROUND["ffo0"]), "ffo0": (C, ROUND["att5"]),
                    "att5": (C, ROUND["att6"]), "att6": (C, ROUND["att_out"]), "att_out": (C, ROUND["ffi1"]),
                    "ffi1": (KH, ROUND["ffo1"]), "ffo1": None, "ffi2": (KH, ROUND["ffo2"]), "ffo2": None}[name]

        def kc_of(name):
            return KH if name.startswith("ffo") else C

        def phase_splits(name, eng, step, evac):
            kc, nxt = kc_of(name), follow(name)
            uniform = nxt is not None and nxt[0] == kc

            def body(g, last):
                for t in range(4):
                    n = N0[name] + 4 * g + t
                    if t < 2:
                        step(n + 2, t % 2, t + 2, kc, ROUND[name] + g)
                    elif not last:
                        step(n + 2, t % 2, t - 2, kc, ROUND[name] + g + 1)
                    elif nxt is not None:
                        step(n + 2, t % 2, t - 2, nxt[0], nxt[1])
                    evac(g, t)
            groups(eng, G[name], uniform, body)

        def act_step(n, par, s, kc, rnd):
            split_hi(n, par, s, kc, rnd)

        def dve_step(n, par, s, kc, rnd):
            split_lo(n, par, s, kc)

        def block(n, par, kc, hi, lo, k0, bank, start, stop, ready=None, between=None):
            pe_ = nc.tensor
            pe_.wait_ge(wlo, n + 1)
            for k in range(kc):
                if ready is not None:
                    pe_.wait_ge(n_lo, ready + k + 1)
                w_h, w_l = WH[par][:, k * P:(k + 1) * P], WL[par][:, k * P:(k + 1) * P]
                pe_.matmul(bank[:, :], w_h, hi[:, k0 + k, :], start=start and k == 0, stop=False)
                pe_.matmul(bank[:, :], w_h, lo[:, k0 + k, :], start=False, stop=False)
                last = pe_.matmul(bank[:, :], w_l, hi[:, k0 + k, :], start=False, stop=stop and k == kc - 1)
                if between is not None and k < kc - 1:
                    between(k)
            last.then_inc(mm, 1)

        def pe_phase(name, hi, lo, ready):
            with nc.tensor.Fori(0, G[name]) as g:
                for t in range(4):
                    nc.tensor.wait_ge(ev[t % 2], O0[name] // 2 + 2 * g + t // 2)
                    block(N0[name] + 4 * g + t, t % 2, C, hi, lo, 0, PS[t % 2], True, True,
                          ready if t == 0 else None)

        def pe_down(name, hid_ready):
            with nc.tensor.Fori(0, G[name]) as g:
                for t in range(4):
                    if t % 2 == 0:
                        nc.tensor.wait_ge(ev[t // 2], O0[name] // 2 + g)
                    nc.tensor.wait_ge(hid_ready, KH * (t % 2 + 1))
                    block(N0[name] + 4 * g + t, t % 2, KH, FH, FL, KH * (t % 2), PS[t // 2],
                          t % 2 == 0, t % 2 == 1)

        def pe_sum(nj_):
            nc.tensor.wait_ge(n_acc, nj_.acc_end)
            for i in range(TC):
                m = nc.tensor.matmul(NS[:, i:i + 1], ACC[:, i * P:(i + 1) * P], ONE[:, 0:1], start=True, stop=True)
            m.then_inc(n_used, 1)

        def pe_bcast(nj_):
            nc.tensor.wait_ge(n_dg, nj_.count)
            nc.tensor.matmul(RB[:, :], ONE[:, :], DG, start=True, stop=True).then_inc(n_rb, 1)

        def dve_mean(nj_, width):
            nc.vector.wait_ge(n_used, nj_.used + 1)
            nc.vector.tensor_scalar(STAT[:, 0:4], NS[:, 0:4], 1.0 / width, EPS, ALU.mult, ALU.add).then_inc(n_ms, 1)

        def dve_diag(nj_, width, mean=True):
            if mean:
                dve_mean(nj_, width)
            nc.vector.wait_ge(n_rs, nj_.count)
            nc.vector.tensor_tensor(DG.rearrange("p (i t) -> p i t", i=TC),
                                    IDN[:, :].rearrange("p (i t) -> p i t", i=1).to_broadcast([P, TC, P]),
                                    STAT[:, 4:8].rearrange("p (i t) -> p i t", t=1).to_broadcast([P, TC, P]),
                                    ALU.mult).then_inc(n_dg, 1)

        def pool_rsqrt(nj_):
            nc.gpsimd.wait_ge(n_ms, nj_.count)
            nc.gpsimd.tensor_tensor(STAT[:, 4:8], STAT[:, 0:4], NHALF[:, 0:4], ALU.pow).then_inc(n_rs, 1)

        def sq_p1(k):
            return (U if k < CA else V)[:, k % CA, :]

        def sq_m(k):
            return M[:, k, :]

        def act_squares(nj_, K, src, ready, dst):
            for k in range(K):
                ready(k)
                nc.scalar.activation(dst(k), src(k), ACT.Square).then_inc(n_sq, 1)

        def pool_sum(nj_, K, sq):
            nc.gpsimd.wait_ge(n_sq, nj_.sq + 1)
            for k in range(1, K):
                nc.gpsimd.wait_ge(n_sq, nj_.sq + k + 1)
                if k > 1:
                    nc.gpsimd.wait_ge(n_acc, nj_.acc + k - 1)
                nc.gpsimd.tensor_tensor(ACC, sq(k), sq(0) if k == 1 else ACC, ALU.add).then_inc(n_acc, 1)

        def act_parts(nj_, K, k0=0, shift=None):
            for k in range(K):
                nc.scalar.wait_ge(n_t, nj_.t + k + 1)
                if shift is None:
                    nc.scalar.activation(HH[:, k0 + k, :], TMP[:, k % 2, :], ACT.Copy).then_inc(n_hi, 1)
                else:
                    nc.scalar.activation(HH[:, k0 + k, :], TMP[:, k % 2, :], ACT.Identity,
                                         bias=shift(k)).then_inc(n_hi, 1)

        def dve_parts(nj_, K, src, gain, k0=0, shift=None):
            nc.vector.wait_ge(n_rb, nj_.count)

            def low(k):
                nc.vector.wait_ge(n_hi, nj_.hi + k + 1)
                hi = HH[:, k0 + k, :].bitcast(F32)
                if shift is None:
                    nc.vector.tensor_tensor(HL[:, k0 + k, :], TMP[:, k % 2, :], hi, ALU.subtract).then_inc(n_lo, 1)
                else:
                    nc.vector.scalar_tensor_tensor(HL[:, k0 + k, :], TMP[:, k % 2, :], shift(k), hi, ALU.add,
                                                   ALU.subtract).then_inc(n_lo, 1)
            for k in range(K):
                if k >= 2:
                    nc.vector.wait_ge(n_lo, nj_.lo + k - 1)
                nc.vector.scalar_tensor_tensor(TMP[:, k % 2, :], src(k), gain(k), RB[:, :], ALU.mult,
                                               ALU.mult).then_inc(n_t, 1)
                if k >= 1:
                    low(k - 1)
            low(K - 1)

        def vcol(name, k):
            return VEC[:, COL[name] + k:COL[name] + k + 1]

        def dve_clear_acc(nj_):
            nc.vector.memset(ACC, 0.0).then_inc(n_acc, 1)

        def dve_gated(nj_, name, m, b, gate0):
            cnt = O0[name] // 2
            nc.vector.wait_ge(mm, m[1])
            nc.vector.scalar_tensor_tensor(X[:, bass.ds(m[0], 1), :], PS[b][:, :].rearrange("p (a s) -> p a s", a=1),
                                           MOD[:, bass.ds(gate0 + m[0], 1)], X[:, bass.ds(m[0], 1), :],
                                           ALU.mult, ALU.add).then_inc(ev[b], 1)
            nc.vector.wait_ge(n_sq, nj_.sq + m[0] + 1)
            nc.vector.wait_ge(n_acc, nj_.acc + m[0] + 1)
            nc.vector.tensor_tensor(ACC, ACC, TMP[:, b, :], ALU.add).then_inc(n_acc, 1)

        def act_gated(nj_, name, m, b, half):
            nc.scalar.wait_ge(ev[b], O0[name] // 2 + half + 1)
            nc.scalar.activation(TMP[:, b:b + 1, :], X[:, bass.ds(m, 1), :], ACT.Square).then_inc(n_sq, 1)

        def act_m(nj_, name, m, b, done, gain, sqscale=None):
            nc.scalar.wait_ge(mm, done)
            nc.scalar.activation(M[:, bass.ds(m, 1), :], PS[b][:, :].rearrange("p (a s) -> p a s", a=1), ACT.Copy,
                                 scale=gain)
            nc.scalar.wait_ge(n_acc, nj_.acc + m)
            if sqscale is None:
                nc.scalar.activation(TMP[:, b, :], PS[b][:, :], ACT.Square).then_inc(ev[b], 1)
            else:
                nc.scalar.activation(TMP[:, b, :], PS[b][:, :], ACT.Square, scale=sqscale).then_inc(ev[b], 1)

        def dve_m(nj_, name, m, b, half):
            nc.vector.wait_ge(ev[b], O0[name] // 2 + half + 1)
            nc.vector.wait_ge(n_acc, nj_.acc + m + 1)
            nc.vector.tensor_tensor(ACC, ACC, TMP[:, b, :], ALU.add).then_inc(n_acc, 1)

        def dve_add_normed(nj_, xs):
            nc.vector.wait_ge(n_rb, nj_.count)

            def add(k):
                nc.vector.wait_ge(n_t, nj_.t + k + 1)
                nc.vector.tensor_tensor(X[:, k, :], X[:, k, :], TMP[:, k % 2, :], ALU.add).then_inc(xs, 1)
            for k in range(C):
                if k >= 2:
                    nc.vector.wait_ge(xs, k - 1)
                nc.vector.tensor_tensor(TMP[:, k % 2, :], M[:, k, :], RB[:, :], ALU.mult).then_inc(n_t, 1)
                if k >= 1:
                    add(k - 1)
            add(C - 1)

        ff = [{k: sem(f"ffn{j}_{k}") for k in ("hid_hi", "hid_lo")} for j in range(3)]
        xs = [sem(f"x_renewed{j}") for j in range(5)]

        def act_ffi(name, s, g, t):
            j, o = 2 * g + t // 2, O0[name] // 2 + 2 * g + t // 2
            if t % 2 == 0:
                nc.scalar.wait_ge(mm, N0[name] + 4 * g + t + 1)
                nc.scalar.activation(TMP[:, t // 2, :], PS[0][:, :], ACT.Silu).then_inc(ev[0], 1)
            else:
                nc.scalar.wait_ge(ev[1], o + 1)
                nc.scalar.activation(FH[:, bass.ds(j, 1), :], TMP2[:, t // 2:t // 2 + 1, :],
                                     ACT.Copy).then_inc(s["hid_hi"], 1)

        def dve_ffi(name, s, g, t):
            j, o = 2 * g + t // 2, O0[name] // 2 + 2 * g + t // 2
            if t % 2 == 1:
                nc.vector.wait_ge(mm, N0[name] + 4 * g + t + 1)
                nc.vector.wait_ge(ev[0], o + 1)
                nc.vector.wait_ge(wlo, N0[name] + 4 * g + t + 2)
                nc.vector.tensor_tensor(TMP2[:, t // 2, :], TMP[:, t // 2, :], PS[1][:, :],
                                        ALU.mult).then_inc(ev[1], 1)
                nc.vector.wait_ge(s["hid_hi"], j + 1)
                nc.vector.tensor_tensor(FL[:, bass.ds(j, 1), :], TMP2[:, t // 2:t // 2 + 1, :],
                                        FH[:, bass.ds(j, 1), :].bitcast(F32), ALU.subtract).then_inc(s["hid_lo"], 1)

        j1 = {k: sem("p1_" + k) for k in (
            "y", "vt", "vtc", "bn", "bna", "msv", "rsv", "ln1", "ln", "conv", "gm", "xc", "sq", "var", "v32", "sd", "rc",
            "r8t", "r8", "gb", "gx", "yb", "sp", "ya1", "ya")}
        a5 = {k: sem("a5_" + k) for k in (
            "xf", "abs", "ex", "lnx", "lf", "cs", "ct", "ctc", "ngt", "ngc", "hc", "g0", "g1t", "g1", "kc2", "kcf",
            "vcf", "vct", "vctc", "vt", "vtc")}
        a6 = {k: sem("a6_" + k) for k in (
            "csel", "cb", "fb", "fbm", "stg", "fvt", "fvc", "qk", "sc", "ex", "cm", "mx", "rc", "rg", "nm",
            "tr", "pt", "pv", "of", "oh", "ol")}
        p10 = {k: sem("p10_" + k) for k in ("u", "z", "cs", "d", "e", "h", "in", "inv")}

        ORDER = [(i, half) for pair in ((3, 0), (2, 1)) for half in range(2) for i in pair]
        KIND = ("fox", "cmp", "slc", "win")

        def item(x):
            g, j = divmod(x, 4)
            i, half = ORDER[g]
            return KIND[j], i, half, (NCMP if j == 1 else (i + 1) * P)

        def foff(i):
            return (0, P, 3 * P, 6 * P)[i]

        blk = ctx.enter_context(nc.Block())

        @blk.sync
        def _(sp):
            sp.dma_start(VEC[:, :], vec).then_inc(ld_vec, 16)

            def load(s, src, width):
                sp.dma_start(RAW[s][:, 0:width], src).then_inc(ld[s], 16)

            def ada_block(i):
                return ada_w[bass.ds(i, 1), :, :].rearrange("a p n -> (a p) n")

            for s in range(4):
                load(s, ada_w[s], D)
            sp.dma_start(X[:, :, :], xT).then_inc(ld_x, 16)
            with sp.Fori(1, 4) as r:
                for s in range(4):
                    sp.wait_ge(raw_used, 4 * (r - 1) + s + 1)
                    load(s, ada_block(4 * r + s), D)
            def load_ada(i, src):
                sp.dma_start(AWB[:, i % 4, :], src).then_inc(ld_ada[i % 4], 16)
            for s in range(4):
                sp.wait_ge(raw_used, ADA_A - 3 + s)
                load(s, w_in[s], D)
                load_ada(s, ada_w[ADA_A + s])
            with sp.Fori(0, 3) as q:
                for t in range(4):
                    sp.wait_ge(wlo, 4 * q + t + 1)
                    load(t, w_in[bass.ds(4 * q + t + 4, 1), :, :].rearrange("a p n -> (a p) n"), D)
                    for i in range(PER * t, PER * t + PER):
                        sp.wait_ge(ada_used, 4 * PER * q + i + 1)
                        load_ada(i, ada_block(4 * PER * q + i + ADA_A + 4))
            for t in range(4):
                sp.wait_ge(wlo, 13 + t)
                load(t, w_out[t], C * P)
                for i in range(12 * PER + 4 + PER * t, min(12 * PER + 4 + PER * (t + 1), ADA_B)):
                    sp.wait_ge(ada_used, i - 3)
                    load_ada(i, ada_w[ADA_A + i])
            sp.dma_start(LNR[:, :, :], ln_rows.rearrange("(o a) n -> o a n", o=1).to_broadcast([P, 2, DA])).then_inc(ld_ln, 16)
            sp.dma_start(WS[:, :, :], ws).then_inc(ld_ws, 16)
            for h in range(HA):
                half = h % 2
                sp.dma_start(BS[64 * half:64 * half + 64, h // 2, :], bs[h:h + 1, :].to_broadcast([64, P])).then_inc(ld_bs, 16)

            def stream(name, src, width, base=0, first=0):
                with sp.Fori(first, G[name]) as g:
                    for s in range(4):
                        sp.wait_ge(wlo, N0[name] + 4 * g + s - 3)
                        load(s, src[bass.ds(base + 4 * g + s, 1), :, :].rearrange("a p n -> (a p) n"), width)

            stream("w_out", w_out, C * P, first=1)
            stream("ffi0", ffi, C * P)
            stream("ffo0", ffo, KH * P)
            stream("att5", att_w, C * P)
            stream("att6", att_w, C * P, base=8)
            stream("att_out", att_out, C * P)
            stream("ffi1", f2i, C * P)
            stream("ffo1", f2o, KH * P)
            for s in range(4):
                sp.wait_ge(wlo, N0["ffi2"] - 3 + s)
                load(s, pool_w[s], 4 * P)
            for s in range(4):
                sp.wait_ge(raw_used, ADA_A + s + 1)
                load(s, f2i[44 + s], C * P)
            stream("ffi2", f2i, C * P, base=44, first=1)
            stream("ffo2", f2o, KH * P, base=16)
            for k in range(C):
                sp.wait_ge(xs[4], k + 1)
                sp.dma_start(outT[:, k, :], X[:, k, :]).then_inc(store_done, 16)
            sp.wait_ge(store_done, 16 * C)

        @blk.gpsimd
        def _(pool):
            cnt = [0]

            def chain(ins):
                cnt[0] += 1
                ins.then_inc(pool_chain, 1)
                pool.wait_ge(pool_chain, cnt[0])

            chain(pool.memset(IDN[:, :], 0.0))
            chain(pool.affine_select(out=IDN[:, :], in_=IDN[:, :], compare_op=ALU.not_equal, fill=1.0, base=0,
                                     pattern=[[-1, P]], channel_multiplier=1))
            chain(pool.memset(NHALF[:, :], -0.5))
            chain(pool.memset(GD[:, :], 0.0))
            for h in range(2):
                chain(pool.memset(GD[64 * h:64 * h + 64, 64 * h:64 * h + 64], 1.0 / 64))
            chain(pool.memset(GSEL[:, :], 0.0))
            for h in range(2):
                chain(pool.memset(GSEL[64 * h:64 * h + 64, h:h + 1], 1.0 / 64))
            chain(pool.memset(SELG[:, :, :], 0.0))
            sg = SELG[:, :, :].rearrange("g c (h d) -> g c h d", h=2)
            chain(pool.affine_select(out=sg, in_=sg, compare_op=ALU.not_equal, fill=1.0, base=0,
                                     pattern=[[-2, CA], [-1, 2], [0, 64]], channel_multiplier=1))
            chain(pool.memset(Y[:, :, 0:TAPS - 1], 0.0))
            chain(pool.memset(AAC[:, 2:, :], 0.0))
            pool.memset(ONE[:, :], 1.0).then_inc(const_ready, 1)
            for b in range(2):
                pool.sem_inc(ev[b], 1)
            pool_sum(nj["n1"], C, sq_p1)
            pool_rsqrt(nj["n1"])

            with pool.Fori(0, ADA_N - 4) as j:
                acc = AAC[:, bass.ds(2 + j, 1), :].rearrange("p a n -> p (a n)")
                for k in range(C):
                    pool.wait_ge(ada_mul, 8 * j + k + 1)
                    if k:
                        pool.wait_ge(ada_used, 8 * j + k)
                    pool.sem_inc(wait_held, 1)
                    pool.tensor_tensor(acc, AWB[:, k % 4, :], acc, ALU.add).then_inc(ada_used, 1)
            pool.wait_ge(ld_ws, 16)
            pool.affine_select(out=WS[:, :, :], in_=WS[:, :, :], compare_op=ALU.is_ge, fill=0.0, base=0,
                               pattern=[[0, HA], [1, P]], channel_multiplier=-1).then_inc(const_ready, 1)
            pool.wait_ge(j1["msv"], 1)
            pool.tensor_tensor(STAT[:, 12:16], STAT[:, 8:12], NHALF[:, :], ALU.pow).then_inc(j1["rsv"], 1)
            for q, sq in (("na", sq_p1), ("nb", lambda k: VT[:, k, :])):
                pool_sum(nj[q], CA, sq)
                pool_rsqrt(nj[q])
            pool_rsqrt(nj["n2"])
            pool.wait_ge(ada_sum, 6)
            chain(pool.memset(LACC, 0.0))

            def late_load(i, src):
                pool.dma_start(LW[:, i % 2, :], src).then_inc(ld_late[i % 2], 16)
            for i in range(2):
                late_load(i, ada_w[ADA_A + ADA_B + i])
            for i in range(ADA_C):
                w, acc = LW[:, i % 2, :], LACC[:, i // C, :]
                pool.wait_ge(ld_late[i % 2], 16 * (i // 2 + 1))
                pool.tensor_scalar(w, w, CACT[:, i % C:i % C + 1], None, ALU.mult).then_inc(late_mul, 1)
                pool.wait_ge(late_mul, i + 1)
                if i:
                    pool.wait_ge(late_used, i)
                pool.tensor_tensor(acc, w, acc, ALU.add).then_inc(late_used, 1)
                if i + 2 < ADA_C:
                    pool.wait_ge(late_used, i + 1)
                    late_load(i + 2, ada_w[ADA_A + ADA_B + i + 2])
            pool_rsqrt(nj["nf"])
            pool_sum(nj["q0"], C, sq_m)
            pool_rsqrt(nj["q0"])
            pool.dma_start(BF[:, :], bf).then_inc(ld_small, 16)
            for h in range(2):
                pool.dma_start(PEB[64 * h:64 * h + 64, :, :], pe).then_inc(ld_small, 16)
            chain(pool.memset(W1B[:, :, :, :], 0.0))
            chain(pool.memset(W2B[:, :, :], 0.0))
            for h in range(2):
                q = slice(64 * h, 64 * h + 64)
                pool.dma_start(W1B[q, :, :, 64 * h:64 * h + 64], w1).then_inc(ld_att, 16)
                pool.dma_start(W2B[q, :, 64 * h:64 * h + 64], w2).then_inc(ld_att, 16)
            chain(pool.iota(DM[:, :], pattern=[[1, S]], base=-(S - P), channel_multiplier=-1,
                            allow_small_or_imprecise_dtypes=True))
            chain(pool.affine_select(out=DM[:, :], in_=DM[:, :], compare_op=ALU.is_ge, fill=NEG, base=S - P,
                                     pattern=[[-1, S]], channel_multiplier=1))
            chain(pool.iota(DC[:, :, :], pattern=[[-P, TC], [16, NCMP]], base=CMPB - 1, channel_multiplier=-1,
                            allow_small_or_imprecise_dtypes=True))
            chain(pool.affine_select(out=DC[:, :, :], in_=DC[:, :, :], compare_op=ALU.is_ge, fill=NEG,
                                     base=-(CMPB - 1), pattern=[[P, TC], [-16, NCMP]], channel_multiplier=1))
            chain(pool.memset(CM[:, :, :], 1.0))
            chain(pool.affine_select(out=CM[:, :, :], in_=CM[:, :, :], compare_op=ALU.is_ge, fill=0.0,
                                     base=-(CMPB - 1), pattern=[[P, TC], [-16, NCMP]], channel_multiplier=1))
            chain(pool.memset(GTS[:, :, :, :], 1.0))
            for h in range(NH):
                chain(pool.memset(SL[:, h:h + 1], 2.0 ** -(h + 1)))
            pool.memset(STAT[:, 15:16], 0.0).then_inc(const_ready, 1)
            with pool.Fori(0, 4) as it:
                for half in range(2):
                    for i in range(TC):
                        pool.wait_ge(a6["fb"], 8 * it + 4 * half + i + 1)
                        pool.sem_inc(wait_held, 1)
                        dst = FB[:, half, foff(i) + i * P:foff(i) + (i + 1) * P]
                        pool.affine_select(out=dst, in_=dst, compare_op=ALU.is_ge, fill=NEG, base=0,
                                           pattern=[[-1, P]], channel_multiplier=1).then_inc(a6["fbm"], 1)
            for r, q in (("r1", "q1"), ("r2", "q2")):
                pool_rsqrt(nj[r])
                if q == "q2":
                    for w in range(4):
                        chain(pool.iota(PINV[:, w, :], pattern=[[1, 16]], base=1, channel_multiplier=0,
                                        allow_small_or_imprecise_dtypes=True))
                    for w in range(4):
                        chain(pool.tensor_scalar(PINV[:, w, :], PINV[:, w, :], float(2 ** (w + 1)), None, ALU.min))
                    pool.memset(PCS[:, :, 0:16], 0.0).then_inc(p10["z"], 1)
                pool_sum(nj[q], C, sq_m)
                pool_rsqrt(nj[q])
                if q == "q2":
                    for k in range(C):
                        w = 2 ** (k // 2 + 1)
                        pool.wait_ge(p10["cs"], k + 1)
                        if k >= 2:
                            pool.wait_ge(p10["in"], k - 1)
                        pool.tensor_tensor(PTM[:, k % 2, :], PCS[:, k % 2, 16:], PCS[:, k % 2, 16 - w:16 - w + S],
                                           ALU.subtract).then_inc(p10["e"], 1)
            pool_rsqrt(nj["r3"])
            pool_sum(nj["q3"], C, sq_m)
            pool_rsqrt(nj["q3"])
            pool_rsqrt(nj["r4"])

        @blk.tensor
        def _(pe_):
            def ada_sums(j, bank, sem_, count):
                pe_.wait_ge(sem_, count)
                for k in range(C):
                    acc = (AAC[:, j, :] if j < ADA_N - 2 else LACC[:, j - ADA_N + 2, :])[:, k * P:(k + 1) * P]
                    m = pe_.matmul(bank[:, C * j + k:C * j + k + 1], acc, ONE[:, 0:1],
                                   start=True, stop=True)
                m.then_inc(ada_sum, 1)

            pe_.wait_ge(const_ready, 1)
            pe_sum(nj["n1"])
            ada_sums(0, PS[5], raw_used, C)
            pe_bcast(nj["n1"])
            ada_sums(1, PS[5], raw_used, 2 * C)
            with pe_.Fori(0, 4) as g:
                for t in range(4):
                    pe_.wait_ge(ev[t % 2], 2 * g + t // 2 + 1)
                    block(4 * g + t, t % 2, C, HH, HL, 0, PS[t % 2], True, True, nj["n1"].lo if t == 0 else None)
            pe_.wait_ge(ev[0], 7)
            pe_.wait_ge(ev[1], 7)
            for i in range(TC):
                if i >= 2:
                    pe_.wait_ge(j1["vtc"], i - 1)
                for c in range(CA):
                    m = pe_.transpose(PS[2 + i % 2][:, c * P:(c + 1) * P], V[:, c, i * P:(i + 1) * P], IDN[:, :])
                m.then_inc(j1["vt"], 1)
            pe_.wait_ge(const_ready, 2)
            pe_.wait_ge(j1["ln"], TC)
            for c in range(CA):
                if c >= 2:
                    pe_.wait_ge(j1["ya1"], c - 1)
                for i in range(TC):
                    for h in range(2):
                        m = pe_.matmul(PS[2 + c % 2][64 * h:64 * h + 64, i * P:(i + 1) * P],
                                       VT[:, i, (2 * c + h) * 64:(2 * c + h + 1) * 64], WS[:, 2 * c + h, :],
                                       start=True, stop=True)
                m.then_inc(j1["sp"], 1)
            for c in range(CA):
                pe_.wait_ge(j1["conv"], (TAPS + 1) * (c + 1))
                if c >= 2:
                    pe_.wait_ge(j1["xc"], c - 1)
                pe_.matmul(PS[4 + c % 2][:, :], GD[:, :], CV[:, c, :], start=True, stop=True).then_inc(j1["gm"], 1)
            for c in range(CA):
                pe_.wait_ge(j1["sq"], c + 1)
                for i in range(TC):
                    m = pe_.matmul(NS[:, 8 * i + 2 * c:8 * i + 2 * c + 2], TMP[:, c % 2, i * P:(i + 1) * P],
                                   GSEL[:, :], start=True, stop=True)
                m.then_inc(j1["var"], 1)
            pe_.wait_ge(j1["rc"], 1)
            for i in range(TC):
                m = pe_.transpose(RB[0:GB, i * P:(i + 1) * P], R32[:, 2, 8 * i:8 * i + 8], IDN[:, :])
            m.then_inc(j1["r8t"], 1)
            pe_sum(nj["na"])
            pe_.wait_ge(j1["r8"], 1)
            for c in range(CA):
                if c >= 2:
                    pe_.wait_ge(j1["gx"], c - 1)
                pe_.matmul(PS[4 + c % 2][:, :], SELG[:, c, :], R8[:, :], start=True, stop=True).then_inc(j1["gb"], 1)
            pe_.wait_ge(j1["gx"], CA)
            pe_bcast(nj["na"])
            ada_sums(2, PS[5], ada_used, C)
            pe_sum(nj["nb"])
            pe_.wait_ge(n_t, nj["na"].t + CA)
            pe_bcast(nj["nb"])
            with pe_.Fori(0, G["w_out"]) as g:
                for t in range(4):
                    pe_.wait_ge(ev[t % 2], O0["w_out"] // 2 + 2 * g + t // 2)
                    if t == 0:
                        pe_.wait_ge(n_lo, nj["na"].lo + CA)
                        pe_.wait_ge(n_lo, nj["nb"].lo + CA)
                    block(N0["w_out"] + 4 * g + t, t % 2, C, HH, HL, 0, PS[t % 2], True, True)
            for j in range(3, 5):
                ada_sums(j, PS[4], ada_used, C * (j - 1))
            pe_sum(nj["n2"])
            pe_bcast(nj["n2"])
            ada_sums(5, PS[5], ada_used, C * 4)
            pe_phase("ffi0", HH, HL, nj["n2"].lo)
            for j in range(2):
                ada_sums(ADA_N - 2 + j, PS[5], late_used, C * (j + 1))
            pe_down("ffo0", ff[0]["hid_lo"])
            pe_sum(nj["nf"])
            pe_bcast(nj["nf"])
            pe_sum(nj["q0"])
            pe_bcast(nj["q0"])

            def lin(name, g, t, ready=None, between=None):
                pe_.wait_ge(ev[t % 2], O0[name] // 2 + 2 * g + t // 2)
                block(N0[name] + 4 * g + t, t % 2, C, HH, HL, 0, PS[t % 2], True, True, ready, between)

            lin("att5", 0, 0, nj["q0"].lo)
            lin("att5", 0, 1)
            lin("att5", 0, 2)
            pe_.wait_ge(a5["cs"], 1)
            for i in range(TC):
                m = pe_.transpose(PS[4][:, i * P:i * P + NH], LF[:, i * P:(i + 1) * P], IDN[0:NH, 0:NH])
            m.then_inc(a5["ct"], 1)
            pe_.wait_ge(ev[1], O0["att5"] // 2 + 1)
            for i in range(TC):
                m = pe_.transpose(PS[5][:, i * P:i * P + 3 * NH], NG[:, i * P:(i + 1) * P], IDN[0:3 * NH, 0:3 * NH])
            m.then_inc(a5["ngt"], 1)
            lin("att5", 0, 3)
            lin("att5", 1, 0)
            lin("att5", 1, 1)
            def v_turn(dst, bank, wait_for, cnt, done, src):
                pe_.wait_ge(wait_for, cnt)
                for i in range(TC):
                    m = pe_.transpose(bank[:, i * P:(i + 1) * P], src[:, i * P:(i + 1) * P], IDN[:, :])
                m.then_inc(done, 1)
            pe_.wait_ge(a5["ctc"], 2)
            v_turn(VST, PS[4], ev[1], O0["att5"] // 2 + 3, a5["vt"], VF)
            pe_.wait_ge(ld_att, 16 * 4)
            for kv in range(2):
                pe_.wait_ge(ev[kv], O0["att5"] // 2 + 2)

                def hidden(j0, j1_):
                    for j in range(j0, j1_):
                        m = pe_.matmul(PS[2 + kv][0:NCMP, 0:P], KE[:, kv, :, j], W1B[:, kv, j, :], start=(j == 0),
                                       stop=(j == CMPB - 1))
                    return m
                lin("att5", 1, 2 + kv, between=lambda k: hidden(4 * k, 4 * k + 4))
                hidden(CMPB - 4, CMPB).then_inc(a5["hc"], 1)
            for kv in range(2):
                pe_.wait_ge(a5["g0"], kv + 1)
                pe_.transpose(PS[2 + kv][:, 128:128 + NCMP], FQ[0:NCMP, kv * P:(kv + 1) * P],
                              IDN[0:NCMP, 0:NCMP]).then_inc(a5["g1t"], 1)
            for kv in range(2):
                pe_.wait_ge(a5["g1"], kv + 1)
                pe_.matmul(PS[2 + kv][:, 256:256 + NCMP], W2B[:, kv, :], G1[:, kv, :], start=True,
                           stop=True).then_inc(a5["kc2"], 1)
            pe_.wait_ge(a5["kcf"], 2)
            pe_.transpose(PS[2][0:NCMP, 384:384 + P], KCF[:, 1, :], IDN[:, :]).then_inc(a5["vct"], 1)
            v_turn(VWT, PS[5], ev[1], O0["att5"] // 2 + 4, a5["vt"], VF)

            with pe_.Fori(0, 4) as it:
                lin("att6", it, 0)
                lin("att6", it, 1)
                for half in range(2):
                    pe_.wait_ge(a6["csel"], 2 * it + half + 1)
                    pe_.matmul(PS[2 + half][:, :], ONE[0:NH, :], CSEL[:, half, :], start=True,
                               stop=True).then_inc(a6["cb"], 1)
                lin("att6", it, 2)
                lin("att6", it, 3)
                pe_.wait_ge(ev[0], O0["att6"] // 2 + 2 * it + 2)
                for i in range(TC):
                    m = pe_.transpose(PS[4][:, i * P:(i + 1) * P], VF[:, i * P:(i + 1) * P], IDN[:, :])
                m.then_inc(a6["fvt"], 1)
                pe_.wait_ge(ev[1], O0["att6"] // 2 + 2 * it + 2)
                pe_.wait_ge(a6["fbm"], 8 * it + 8)

                def qk(x):
                    kind, i, half, L = item(x)
                    if x >= 4:
                        pe_.wait_ge(a6["sc"], 32 * it + x - 3)
                    q = slice(64 * half, 64 * half + 64)
                    lhs = (FQ if kind == "fox" else NQ)[q, i * P:(i + 1) * P]
                    rhs = {"fox": FK[q, 0:L], "cmp": KCF[q, 0, :], "slc": KS[q, 0:L], "win": KW[q, 0:L]}[kind]
                    pe_.matmul(PS[x % 4][:, 0:L], lhs, rhs, start=True, stop=True).then_inc(a6["qk"], 1)

                def turn(x):
                    kind, i, half, L = item(x)
                    pe_.wait_ge(a6["nm"], 32 * it + x + 1)
                    if x >= 2:
                        pe_.wait_ge(a6["pt"], 32 * it + x - 1)
                    elif x == 0:
                        pe_.wait_ge(a6["fvc"], it + 1)
                    bank = PS[4 + x % 2]
                    if kind == "cmp":
                        m = pe_.transpose(bank[0:NCMP, 0:P], SC[:, x % 8, 0:NCMP], IDN[:, :])
                    else:
                        for j in range(i + 1):
                            m = pe_.transpose(bank[:, j * P:(j + 1) * P], SC[:, x % 8, j * P:(j + 1) * P], IDN[:, :])
                    m.then_inc(a6["tr"], 1)

                def pv(x):
                    kind, i, half, L = item(x)
                    pe_.wait_ge(a6["pt"], 32 * it + x + 1)
                    q = slice(64 * half, 64 * half + 64)
                    bank = PS[6] if kind == "fox" else PS[7]
                    dst = bank[q, i * P:(i + 1) * P]
                    if kind == "cmp":
                        m = pe_.matmul(dst, VCT[:, q], PT[0:NCMP, x % 3, 0:P], start=True, stop=False,
                                       skip_group_check=True)
                    else:
                        vt = {"fox": FVT, "slc": VST, "win": VWT}[kind]
                        for j in range(i + 1):
                            m = pe_.matmul(dst, vt[:, j, q], PT[:, x % 3, j * P:(j + 1) * P],
                                           start=(kind == "fox" and j == 0),
                                           stop=(kind != "slc" and j == i), skip_group_check=True)
                    m.then_inc(a6["pv"], 1)

                for g in range(9):
                    a, b = 4 * g, 4 * g - 4
                    for step, j in (("qk", 0), ("qk", 1), ("turn", 0), ("turn", 1), ("qk", 2), ("qk", 3), ("pv", 0), ("turn", 2), ("pv", 1), ("turn", 3), ("pv", 2), ("pv", 3)):
                        if step == "qk" and g < 8:
                            qk(a + j)
                        elif step == "turn" and g > 0:
                            turn(b + j)
                        elif step == "pv" and g > 0:
                            pv(b + j)
            with pe_.Fori(0, G["att_out"]) as g:
                for t in range(4):
                    if t == 0:
                        pe_.wait_ge(a6["ol"], 8)
                    pe_.wait_ge(ev[t % 2], O0["att_out"] // 2 + 2 * g + t // 2)
                    block(N0["att_out"] + 4 * g + t, t % 2, C, AH, AL, 0, PS[t % 2], True, True)
            pe_sum(nj["r1"])
            pe_bcast(nj["r1"])
            pe_sum(nj["q1"])
            pe_bcast(nj["q1"])
            pe_phase("ffi1", HH, HL, nj["q1"].lo)
            pe_down("ffo1", ff[1]["hid_lo"])
            pe_sum(nj["r2"])
            pe_bcast(nj["r2"])
            pe_sum(nj["q2"])
            pe_bcast(nj["q2"])
            for gr in range(4):
                pe_.wait_ge(ld[gr], 16 * (ROUND["pool"] + 1))
                pe_.wait_ge(p10["in"], 2 * gr + 2)
                for mo in range(2):
                    o = 2 * gr + mo
                    pe_.wait_ge(ev[mo], O0["pool"] // 2 + gr)
                    for k in range(2):
                        m = pe_.matmul(PS[mo][:, :], RAW[gr][:, (2 * mo + k) * P:(2 * mo + k + 1) * P],
                                       PIN[:, 2 * gr + k, :], start=(k == 0), stop=(k == 1))
                    if mo == 0:
                        m.then_inc(p10["d"], 1)
                m.then_inc(raw_used, 1)
            pe_sum(nj["r3"])
            pe_bcast(nj["r3"])
            pe_sum(nj["q3"])
            pe_bcast(nj["q3"])
            pe_phase("ffi2", HH, HL, nj["q3"].lo)
            pe_down("ffo2", ff[2]["hid_lo"])
            pe_sum(nj["r4"])
            pe_bcast(nj["r4"])

        @blk.scalar
        def _(act):
            act.wait_ge(ld_vec, 16)
            act.activation(CACT[:, :], VEC[:, COL["c"]:COL["c"] + C], ACT.Silu).then_inc(c_ready, 1)
            act.wait_ge(ld_x, 16)
            act_squares(nj["n1"], C, lambda k: X[:, k, :], lambda k: None, sq_p1)
            split_hi(0, 0, 0, C, R_P1, first=True)
            split_hi(1, 1, 1, C, R_P1, first=True)
            act_parts(nj["n1"], C, shift=lambda k: MOD[:, k:k + 1])

            def ada_products(i0, n):
                for i in range(i0, i0 + n):
                    act.wait_ge(ld_ada[i % 4], 16 * (i // 4 + 1))
                    act.activation(AWB[:, i % 4, :], AWB[:, i % 4, :], ACT.Copy,
                                   scale=CACT[:, i % C:i % C + 1]).then_inc(ada_mul, 1)
            ada_products(0, 4)
            for n in range(16):
                if n < 14:
                    split_hi(n + 2, n % 2, (n + 2) % 4, C, R_P1 + (n + 2) // 4)
                else:
                    split_hi(n + 2, n % 2, n - 14, C, ROUND["w_out"])
                act.wait_ge(mm, n + 1)
                b, c = n % 2, n // 2
                if n < 8:
                    if n % 2 == 0:
                        act.activation(V[:, c, :], PS[0][:, :], ACT.Identity, bias=vcol("b_in", n)).then_inc(ev[0], 1)
                    else:
                        if c >= 1:
                            act.wait_ge(j1["y"], c)
                        act.activation(SIG[:, :], PS[1][:, :], ACT.Sigmoid, bias=vcol("b_in", n)).then_inc(ev[1], 1)
                elif n < 12:
                    if n == 8:
                        act.wait_ge(j1["y"], CA)
                    act.activation(V[:, n - 8, :], PS[b][:, :], ACT.Gelu, bias=vcol("b_in", n)).then_inc(ev[b], 1)
                else:
                    act.activation(U[:, n - 12, :], PS[b][:, :], ACT.Gelu, bias=vcol("b_in", n)).then_inc(ev[b], 1)
                if PER * n + 4 < ADA_B:
                    ada_products(PER * n + 4, PER)
            for i in range(TC):
                act.wait_ge(j1["vt"], i + 1)
                act.activation(VT[:, i, :], PS[2 + i % 2][:, :], ACT.Copy).then_inc(j1["vtc"], 1)
            act_squares(nj["na"], CA, lambda k: YA[:, k, :], lambda k: act.wait_ge(j1["ya"], k + 1), sq_p1)
            for c in range(CA):
                act.wait_ge(j1["xc"], c + 1)
                if c >= 2:
                    act.wait_ge(j1["var"], c - 1)
                act.activation(TMP[:, c % 2, :], CV[:, c, :], ACT.Square).then_inc(j1["sq"], 1)
            act.wait_ge(j1["v32"], 1)
            act.activation(R32[:, 1, :], R32[:, 0, :], ACT.Sqrt).then_inc(j1["sd"], 1)
            act.wait_ge(j1["r8t"], 1)
            act.activation(R8[:, :], RB[0:GB, :], ACT.Copy).then_inc(j1["r8"], 1)
            for c in range(CA):
                act.wait_ge(j1["gx"], c + 1)
                act.activation(CV[:, c, :], CV[:, c, :], ACT.Silu, bias=vcol("gn_b", c),
                               scale=vcol("gn_g", c)).then_inc(j1["yb"], 1)
            act_squares(nj["nb"], CA, lambda k: CV[:, k, :], lambda k: act.wait_ge(j1["yb"], k + 1), lambda k: VT[:, k, :])
            act_parts(nj["na"], CA)
            act_parts(nj["nb"], CA, k0=CA)
            phase_splits("w_out", act, act_step,
                         lambda g, t: act_gated(nj["n2"], "w_out", 4 * g + t, t % 2, 2 * g + t // 2))
            act_parts(nj["n2"], C, shift=lambda k: MOD[:, 24 + k:25 + k])
            phase_splits("ffi0", act, act_step, lambda g, t: act_ffi("ffi0", ff[0], g, t))
            phase_splits("ffo0", act, act_step,
                         lambda g, t: act_gated(nj["nf"], "ffo0", 2 * g + t // 2, t // 2, g) if t % 2 else None)
            act_squares(nj["q0"], C, lambda k: X[:, k, :], lambda k: act.wait_ge(xs[0], k + 1), sq_m)
            act_parts(nj["q0"], C)

            def evac5(g, t):
                act.wait_ge(mm, N0["att5"] + 4 * g + t + 1)
                bank, b = PS[t % 2], t % 2
                if (g, t) == (0, 0):
                    act.wait_ge(ld_small, 16 * 3)
                    act.activation(LX, bank[0:NH, :], ACT.Identity, bias=BF[:, 0:1]).then_inc(ev[b], 1)
                    act.wait_ge(a5["abs"], 1)
                    act.activation(LE, LA, ACT.Exp, scale=-1.0).then_inc(a5["ex"], 1)
                    act.wait_ge(a5["ex"], 1)
                    act.activation(LA, LE, ACT.Ln, bias=1.0).then_inc(a5["lnx"], 1)
                elif (g, t) == (0, 1):
                    act.activation(NG, bank[0:3 * NH, :], ACT.Sigmoid).then_inc(ev[b], 1)
                elif (g, t) == (1, 0):
                    act.activation(KS[:, :], bank[:, :], ACT.Copy).then_inc(ev[b], 1)
                elif (g, t) == (1, 1):
                    act.activation(VF[:, :], bank[:, :], ACT.Copy).then_inc(ev[b], 1)
                    act.wait_ge(a5["vt"], 1)
                    act.activation(VST[:, :, :], PS[4][:, :].rearrange("p (a b) -> p a b", a=TC), ACT.Copy).then_inc(a5["vtc"], 1)
                elif (g, t) == (1, 2):
                    act.activation(KW[:, :], bank[:, :], ACT.Copy).then_inc(ev[b], 1)
                elif (g, t) == (1, 3):
                    act.activation(VF[:, :], bank[:, :], ACT.Copy).then_inc(ev[b], 1)
                    for kv in range(2):
                        act.wait_ge(a5["hc"], kv + 1)
                        act.activation(FQ[0:NCMP, kv * P:(kv + 1) * P], PS[2 + kv][0:NCMP, 0:P],
                                       ACT.Gelu_apprx_tanh).then_inc(a5["g0"], 1)
                    for kv in range(2):
                        act.wait_ge(a5["g1t"], kv + 1)
                        act.activation(G1[:, kv, :], PS[2 + kv][:, 128:128 + NCMP], ACT.Copy).then_inc(a5["g1"], 1)
                    for kv in range(2):
                        act.wait_ge(a5["kc2"], kv + 1)
                        act.activation(KCF[:, kv, :], PS[2 + kv][:, 256:256 + NCMP], ACT.Copy).then_inc(a5["kcf"], 1)
                    act.wait_ge(a5["vct"], 1)
                    act.activation(VCT[:, :], PS[2][0:NCMP, 384:384 + P], ACT.Copy).then_inc(a5["vctc"], 1)
                    act.wait_ge(a5["vt"], 2)
                    act.activation(VWT[:, :, :], PS[5][:, :].rearrange("p (a b) -> p a b", a=TC), ACT.Copy).then_inc(a5["vtc"], 1)
            for g in range(2):
                for t in range(4):
                    split_hi(N0["att5"] + 4 * g + t + 2, t % 2, (t + 2) % 4, C, ROUND["att5"] + g + (t >= 2))
                    evac5(g, t)

            def fox_bias(it):
                for half in range(2):
                    act.wait_ge(a6["cb"], 2 * it + half + 1)
                    for i in range(TC):
                        act.activation(FB[:, half, foff(i):foff(i) + (i + 1) * P], PS[2 + half][:, 0:(i + 1) * P],
                                       ACT.Identity, bias=CTS[:, i, half:half + 1], scale=-1.0).then_inc(a6["fb"], 1)

            def heads(it):
                act.wait_ge(a6["fvt"], it + 1)
                act.activation(FVT[:, :, :], PS[4][:, :].rearrange("p (a b) -> p a b", a=TC), ACT.Copy).then_inc(a6["fvc"], 1)

                def exp(x):
                    kind, i, half, L = item(x)
                    act.wait_ge(a6["sc"], 32 * it + x + 1)
                    if kind == "cmp":
                        act.activation(SC[:, x % 8, 0:L], SC[:, x % 8, 0:L], ACT.Exp, scale=-1.0,
                                       bias=AST[:, 0, x:x + 1]).then_inc(a6["ex"], 1)
                    else:
                        act.activation(SC[:, x % 8, 0:L], SC[:, x % 8, 0:L], ACT.Exp, scale=-1.0,
                                       bias=AST[:, 0, x:x + 1], accum_out=AST[:, 1, x:x + 1]).then_inc(a6["ex"], 1)

                def take(x):
                    kind, i, half, L = item(x)
                    act.wait_ge(a6["tr"], 32 * it + x + 1)
                    if x >= 3:
                        act.wait_ge(a6["pv"], 32 * it + x - 2)
                    if kind == "cmp":
                        act.activation(PT[0:NCMP, x % 3, 0:P], PS[4 + x % 2][0:NCMP, 0:P], ACT.Copy).then_inc(a6["pt"], 1)
                    else:
                        act.activation(PT[:, x % 3, 0:L], PS[4 + x % 2][:, 0:L], ACT.Copy).then_inc(a6["pt"], 1)
                for g in range(9):
                    for j in (0, 2):
                        for x in (j, j + 1):
                            if g < 8:
                                exp(4 * g + x)
                        for x in (j, j + 1):
                            if g > 0:
                                take(4 * g - 4 + x)
                act.wait_ge(a6["pv"], 32 * it + 32)
                act.activation(AH[:, bass.ds(it, 1), :], PS[6][:, :].rearrange("p (a s) -> p a s", a=1),
                               ACT.Copy).then_inc(a6["oh"], 1)
                act.activation(AH[:, bass.ds(it + 4, 1), :], PS[7][:, :].rearrange("p (a s) -> p a s", a=1),
                               ACT.Copy).then_inc(a6["oh"], 1)

            def evac6(g, t):
                act.wait_ge(mm, N0["att6"] + 4 * g + t + 1)
                bank, b = PS[t % 2], t % 2
                dst = (FQ, FK, VF, NQ)[t]
                act.activation(dst[:, :], bank[:, :], ACT.Copy, scale=(1.0, 0.125)[t in (0, 3)]).then_inc(ev[b], 1)
                if t == 1:
                    fox_bias(g)
                if t == 3:
                    heads(g)
            phase_splits("att6", act, act_step, evac6)

            def m_phase(name, r, norm_col):
                if name.startswith("ffo"):
                    phase_splits(name, act, act_step, lambda g, t: act_m(
                        nj[r], name, 2 * g + t // 2, t // 2, N0[name] + 4 * g + t + 1,
                        VEC[:, bass.ds(COL["norm_g2"] + norm_col + 2 * g + t // 2, 1)]) if t % 2 else None)
                else:
                    phase_splits(name, act, act_step, lambda g, t: act_m(
                        nj[r], name, 4 * g + t, t % 2, N0[name] + 4 * g + t + 1,
                        VEC[:, bass.ds(COL["norm_g2"] + norm_col + 4 * g + t, 1)]))

            m_phase("att_out", "r1", 8)
            act_squares(nj["q1"], C, lambda k: X[:, k, :], lambda k: act.wait_ge(xs[1], k + 1), sq_m)
            act_parts(nj["q1"], C)
            phase_splits("ffi1", act, act_step, lambda g, t: act_ffi("ffi1", ff[1], g, t))
            m_phase("ffo1", "r2", 24)
            act_squares(nj["q2"], C, lambda k: X[:, k, :], lambda k: act.wait_ge(xs[2], k + 1), sq_m)
            for o in range(C):
                gr, mo = divmod(o, 2)
                if mo == 0:
                    act.wait_ge(p10["d"], gr + 1)
                else:
                    act.wait_ge(raw_used, ADA_A + gr + 1)
                act.activation(M[:, o, :], PS[mo][:, :], ACT.Copy, scale=PG[:, o:o + 1])
                act.wait_ge(n_acc, nj["r3"].acc + o)
                act.activation(TMP[:, mo, :], PS[mo][:, :], ACT.Square, scale=vcol("pool_s", o)).then_inc(ev[mo], 1)
            split_hi(N0["ffi2"], 0, 0, C, ROUND["ffi2"])
            split_hi(N0["ffi2"] + 1, 1, 1, C, ROUND["ffi2"])
            act_squares(nj["q3"], C, lambda k: X[:, k, :], lambda k: act.wait_ge(xs[3], k + 1), sq_m)
            act_parts(nj["q3"], C)
            phase_splits("ffi2", act, act_step, lambda g, t: act_ffi("ffi2", ff[2], g, t))
            m_phase("ffo2", "r4", 56)

        @blk.vector
        def _(dve):
            dve.memset(AAC[:, 0:2, :], 0.0).then_inc(mod_ready, 1)
            dve.wait_ge(mod_ready, 1)
            dve.wait_ge(c_ready, 1)
            for i in range(ADA_A):
                dve.wait_ge(ld[i % 4], 16 * (i // 4 + 1))
                if i:
                    dve.wait_ge(raw_used, i)
                j, k = divmod(i, C)
                dve.scalar_tensor_tensor(AAC[:, j, :], RAW[i % 4][:, 0:D], CACT[:, k:k + 1], AAC[:, j, :], ALU.mult,
                                         ALU.add).then_inc(raw_used, 1)
                if i == ADA_A - 4:
                    dve.wait_ge(const_ready, 1)
                    dve_diag(nj["n1"], D)
            split_lo(0, 0, 0, C)
            split_lo(1, 1, 1, C)
            dve.wait_ge(ada_sum, 2)
            dve.tensor_tensor(MOD[:, 0:16], PS[5][:, 0:16], VEC[:, COL["ada_b"]:COL["ada_b"] + 16], ALU.add).then_inc(mod_ready, 1)
            dve.wait_ge(mod_ready, 2)

            def gain(slot, scale0, norm):
                return dve.scalar_tensor_tensor(GS[:, slot, :], MOD[:, scale0:scale0 + C], 1.0,
                                                VEC[:, COL[norm]:COL[norm] + C], ALU.add, ALU.mult)
            gain(0, 8, "norm1").then_inc(mod_ready, 1)
            dve.wait_ge(mod_ready, 3)
            dve_parts(nj["n1"], C, lambda k: X[:, k, :], lambda k: GS[:, 0, k:k + 1], shift=lambda k: MOD[:, k:k + 1])
            taps = [(c, k) for c in range(CA) for k in range(TAPS + 1)]
            done = [0]

            def tap():
                c, k = taps[done[0]]
                w = VEC[:, COL["conv_w"] + TAPS * c + k:COL["conv_w"] + TAPS * c + k + 1]
                dst = CV[:, c, :] if k % 2 == 0 else TMP[:, c % 2, :]
                if done[0] >= 2:
                    dve.wait_ge(j1["conv"], done[0] - (1 if k < TAPS else 0))
                if k == 0:
                    ins = dve.tensor_scalar(dst, Y[:, c, 0:S], w, vcol("conv_b", c), ALU.mult, ALU.add)
                elif k == 1:
                    ins = dve.tensor_scalar(dst, Y[:, c, 1:1 + S], w, None, ALU.mult)
                elif k < TAPS:
                    ins = dve.scalar_tensor_tensor(dst, Y[:, c, k:k + S], w, dst, ALU.mult, ALU.add)
                else:
                    ins = dve.tensor_tensor(CV[:, c, :], CV[:, c, :], TMP[:, c % 2, :], ALU.add)
                ins.then_inc(j1["conv"], 1)
                done[0] += 1

            for n in range(16):
                if n < 14:
                    split_lo(n + 2, n % 2, (n + 2) % 4, C)
                else:
                    split_lo(n + 2, n % 2, n - 14, C)
                if n < 8 and n % 2:
                    c = n // 2
                    dve.wait_ge(ev[1], c + 2)
                    dve.tensor_tensor(Y[:, c, TAPS - 1:], V[:, c, :], SIG[:, :], ALU.mult).then_inc(j1["y"], 1)
                    dve.wait_ge(j1["y"], c + 1)
                if n >= 1:
                    for _ in range(DVE_TAPS):
                        if done[0] < len(taps) and (n >= 7 or taps[done[0]][0] <= (n - 1) // 2):
                            tap()
            for i in range(TC):
                dve.wait_ge(j1["vtc"], i + 1)
                dve.bn_stats(BN[:, i, :], VT[:, i, :]).then_inc(j1["bn"], 1)
            for i in range(TC):
                dve.wait_ge(j1["bn"], i + 1)
                dve.bn_aggr(MV[:, i, :], BN[:, i, :]).then_inc(j1["bna"], 1)
            dve.wait_ge(j1["bna"], TC)
            dve.tensor_scalar(STAT[:, 8:12], MV[:, :, 1], EPS, None, ALU.add).then_inc(j1["msv"], 1)
            for _ in range(2):
                tap()
            dve.wait_ge(ld_ln, 16)
            dve.wait_ge(j1["rsv"], 1)
            for i in range(TC):
                dve.scalar_tensor_tensor(VT[:, i, :], VT[:, i, :], MV[:, i, 0:1], LNR[:, 0, :], ALU.subtract,
                                         ALU.mult).then_inc(j1["ln1"], 1)
            for i in range(TC):
                dve.wait_ge(j1["ln1"], i + 1)
                dve.scalar_tensor_tensor(VT[:, i, :], VT[:, i, :], STAT[:, 12 + i:13 + i], LNR[:, 1, :], ALU.mult,
                                         ALU.add).then_inc(j1["ln"], 1)
            while done[0] < len(taps):
                tap()
            dve.wait_ge(ld_bs, 16 * HA)
            dve.wait_ge(ev[0], 9)
            dve.wait_ge(ev[1], 9)
            for c in range(CA):
                dve.wait_ge(j1["sp"], c + 1)
                dve.tensor_tensor(YA[:, c, :].rearrange("p (i t) -> p i t", i=TC),
                                  PS[2 + c % 2][:, :].rearrange("p (i t) -> p i t", i=TC),
                                  BS[:, c:c + 1, :].to_broadcast([P, TC, P]), ALU.add).then_inc(j1["ya1"], 1)
                dve.wait_ge(j1["ya1"], c + 1)
                dve.tensor_tensor(YA[:, c, :], YA[:, c, :], U[:, c, :], ALU.mult).then_inc(j1["ya"], 1)
            for c in range(CA):
                dve.wait_ge(j1["gm"], c + 1)
                dve.tensor_tensor(CV[:, c, :], CV[:, c, :], PS[4 + c % 2][:, :], ALU.subtract).then_inc(j1["xc"], 1)
            dve.wait_ge(j1["var"], CA)
            dve.tensor_scalar(R32[:, 0, :], NS[:, 0:32], EPS, None, ALU.add).then_inc(j1["v32"], 1)
            dve.wait_ge(j1["sd"], 1)
            dve.reciprocal(R32[:, 2, :], R32[:, 1, :]).then_inc(j1["rc"], 1)
            for c in range(CA):
                dve.wait_ge(j1["gb"], c + 1)
                dve.tensor_tensor(CV[:, c, :], CV[:, c, :], PS[4 + c % 2][:, :], ALU.mult).then_inc(j1["gx"], 1)
                if c == 0:
                    dve_mean(nj["na"], DA)
            dve_diag(nj["na"], DA, mean=False)
            dve_parts(nj["na"], CA, lambda k: YA[:, k, :], lambda k: vcol("on_a", k))
            dve_diag(nj["nb"], DA)
            dve_parts(nj["nb"], CA, lambda k: CV[:, k, :], lambda k: vcol("on_b", k), k0=CA)
            dve_clear_acc(nj["n2"])
            dve.wait_ge(ada_sum, 3)
            dve.tensor_tensor(MOD[:, 16:24], PS[5][:, 16:24], VEC[:, COL["ada_b"] + 16:COL["ada_b"] + 24], ALU.add).then_inc(mod_ready, 1)
            dve.tensor_tensor(PG[:, :], VEC[:, COL["pool_s"]:COL["pool_s"] + C],
                              VEC[:, COL["norm_g2"] + 40:COL["norm_g2"] + 48], ALU.mult).then_inc(mod_ready, 1)
            dve.wait_ge(mod_ready, 5)
            phase_splits("w_out", dve, dve_step, lambda g, t: dve_gated(
                nj["n2"], "w_out", (4 * g + t, N0["w_out"] + 4 * g + t + 1), t % 2, 16))
            dve.wait_ge(ada_sum, 5)
            dve.tensor_tensor(MOD[:, 24:40], PS[4][:, 24:40], VEC[:, COL["ada_b"] + 24:COL["ada_b"] + 40], ALU.add).then_inc(mod_ready, 1)
            dve_mean(nj["n2"], D)
            dve.wait_ge(mod_ready, 6)
            gain(1, 32, "norm2").then_inc(mod_ready, 1)
            dve_diag(nj["n2"], D, mean=False)
            dve.wait_ge(mod_ready, 7)
            dve_parts(nj["n2"], C, lambda k: X[:, k, :], lambda k: GS[:, 1, k:k + 1],
                      shift=lambda k: MOD[:, 24 + k:25 + k])
            dve.wait_ge(ada_sum, 6)
            dve.tensor_tensor(MOD[:, 40:48], PS[5][:, 40:48], VEC[:, COL["ada_b"] + 40:COL["ada_b"] + 48], ALU.add).then_inc(mod_ready, 1)
            phase_splits("ffi0", dve, dve_step, lambda g, t: dve_ffi("ffi0", ff[0], g, t))
            dve.wait_ge(ff[0]["hid_lo"], CF)
            dve.wait_ge(ada_sum, ADA_N)
            dve.tensor_tensor(MOD[:, 48:64], PS[5][:, 48:64], VEC[:, COL["ada_b"] + 48:COL["ada_b"] + 64], ALU.add).then_inc(mod_ready, 1)
            dve.wait_ge(mod_ready, 9)
            gain(2, 56, "normf").then_inc(mod_ready, 1)
            dve.wait_ge(mod_ready, 10)
            dve_clear_acc(nj["nf"])
            phase_splits("ffo0", dve, dve_step, lambda g, t: dve_gated(
                nj["nf"], "ffo0", (2 * g + t // 2, N0["ffo0"] + 4 * g + t + 1), t // 2, 40) if t % 2 else None)
            dve_diag(nj["nf"], D)
            dve.wait_ge(n_rb, nj["nf"].count)
            for k in range(C):
                if k >= 2:
                    dve.wait_ge(xs[0], k - 1)
                dve.scalar_tensor_tensor(TMP[:, k % 2, :], X[:, k, :], GS[:, 2, k:k + 1], RB[:, :], ALU.mult,
                                         ALU.mult).then_inc(n_t, 1)
                dve.wait_ge(n_t, nj["nf"].t + k + 1)
                dve.tensor_scalar(X[:, k, :], TMP[:, k % 2, :], MOD[:, 48 + k:49 + k], None, ALU.add).then_inc(xs[0], 1)
            dve_diag(nj["q0"], D)
            dve.wait_ge(xs[0], C)
            dve_parts(nj["q0"], C, lambda k: X[:, k, :], lambda k: vcol("norm_g2", k))

            def evac5(g, t):
                done_n = N0["att5"] + 4 * g + t + 1
                if (g, t) == (0, 0):
                    dve.wait_ge(ev[0], O0["att5"] // 2 + 1)
                    dve.scalar_tensor_tensor(LA, LX, -1.0, LX, ALU.mult, ALU.max).then_inc(a5["abs"], 1)
                    dve.memset(LF[:, :], 1.0).then_inc(a5["lf"], 1)
                    dve.wait_ge(a5["lnx"], 1)
                    dve.scalar_tensor_tensor(LE, LX, 0.0, LA, ALU.min, ALU.subtract).then_inc(a5["lf"], 1)
                    dve.wait_ge(a5["lf"], 2)
                    dve.tensor_tensor_scan(LF[:, :], ONES_ROW, LE, 0.0, ALU.mult, ALU.add).then_inc(a5["cs"], 1)
                elif t in (2, 3) and g == 0:
                    kv = t - 2
                    dve.wait_ge(mm, done_n)
                    dve.wait_ge(ld_small, 16 * 3)
                    src = PS[t % 2][:, :].rearrange("p (n j) -> p n j", j=16)
                    pe_v = PEB[:, kv:kv + 1, :]
                    dve.tensor_tensor(KE[:, kv, :, 0:16], src[:, 0:NCMP, :], pe_v[:, :, 0:16].to_broadcast([P, NCMP, 16]),
                                      ALU.add)
                    dve.tensor_tensor(KE[:, kv, :, 16:32], src[:, 1:NCMP + 1, :],
                                      pe_v[:, :, 16:32].to_broadcast([P, NCMP, 16]), ALU.add).then_inc(ev[t % 2], 1)
                    if kv == 0:
                        dve.wait_ge(a5["ct"], 1)
                        dve.tensor_copy(CTK[:, :, :], PS[4][:, :].rearrange("p (i t) -> p i t", i=TC)[:, :, 0:NH]).then_inc(a5["ctc"], 1)
                        dve.wait_ge(a5["ngt"], 1)
                        dve.tensor_copy(GT[:, :, :], PS[5][:, :].rearrange("p (i t) -> p i t", i=TC)[:, :, 0:3 * NH]).then_inc(a5["ctc"], 1)
            ONES_ROW = ONE[0:NH, 0:1].to_broadcast([NH, S])
            for g in range(2):
                for t in range(4):
                    split_lo(N0["att5"] + 4 * g + t + 2, t % 2, (t + 2) % 4, C)
                    evac5(g, t)
            dve.wait_ge(a5["ctc"], 2)
            dve.wait_ge(const_ready, 3)
            dve.wait_ge(a5["vtc"], 2)

            def heads(it):
                def score(x):
                    kind, i, half, L = item(x)
                    dve.wait_ge(a6["qk"], 32 * it + x + 1)
                    if x == 0:
                        dve.wait_ge(a6["fbm"], 8 * it + 8)
                    if x >= 8:
                        dve.wait_ge(a6["tr"], 32 * it + x - 7)
                    bias = {"fox": FB[:, half, foff(i):foff(i) + L] if kind == "fox" else None,
                            "cmp": CLB[:, half, i, :]}.get(kind, ALB[:, half, S - L:S])
                    dve.sem_inc(wait_held, 1)
                    dve.tensor_tensor_reduce(SC[:, x % 8, 0:L], PS[x % 4][:, 0:L], bias, -1.0, 3.0e38, ALU.add,
                                             ALU.min, AST[:, 0, x:x + 1]).then_inc(a6["sc"], 1)

                def stats(g):
                    x = 4 * g + 1
                    dve.wait_ge(a6["ex"], 32 * it + x + 1)
                    i = item(x)[1]
                    dve.tensor_tensor_reduce(SC[:, x % 8, 0:NCMP], SC[:, x % 8, 0:NCMP], CM[:, i, :], 1.0, 0.0,
                                             ALU.mult, ALU.add, AST[:, 1, x:x + 1]).then_inc(a6["cm"], 1)
                    dve.wait_ge(a6["ex"], 32 * it + 4 * g + 4)
                    dve.wait_ge(a6["cm"], 8 * it + g + 1)
                    cols = slice(4 * g, 4 * g + 4)
                    dve.tensor_scalar(AST[:, 1, cols], AST[:, 1, cols], 1e-30, None, ALU.max).then_inc(a6["mx"], 1)
                    dve.wait_ge(a6["mx"], 8 * it + g + 1)
                    dve.reciprocal(AST[:, 2, cols], AST[:, 1, cols]).then_inc(a6["rc"], 1)
                    dve.wait_ge(a6["rc"], 8 * it + g + 1)

                def norm(x):
                    kind, i, half, L = item(x)
                    sc = SC[:, x % 8, 0:L]
                    dve.tensor_scalar(sc, sc, AST[:, 2, x:x + 1], GTS[:, i, half, x % 4:x % 4 + 1], ALU.mult,
                                      ALU.mult).then_inc(a6["nm"], 1)
                for g in range(9):
                    a, b = 4 * g, 4 * g - 4
                    if g > 0:
                        stats(g - 1)
                    for step, j in (("norm", 0), ("norm", 1), ("norm", 2), ("score", 0), ("score", 1), ("norm", 3), ("score", 2), ("score", 3)):
                        if step == "norm" and g > 0:
                            norm(b + j)
                        elif step == "score" and g < 8:
                            score(a + j)
                for b in range(2):
                    dve.wait_ge(a6["oh"], 2 * it + b + 1)
                    dve.tensor_tensor(AL[:, bass.ds(it + 4 * b, 1), :], PS[6 + b][:, :].rearrange("p (a s) -> p a s", a=1),
                                      AH[:, bass.ds(it + 4 * b, 1), :].bitcast(F32), ALU.subtract).then_inc(a6["ol"], 1)

            def evac6(g, t):
                if t == 0:
                    dve.tensor_copy(CTS[:, :, :], CTK[:, :, bass.ds(2 * g, 2)]).then_inc(a6["stg"], 1)
                    for half in range(2):
                        h = 2 * g + half
                        dve.tensor_scalar(CSEL[:, half, :], LF[:, :], IDN[0:NH, bass.ds(h, 1)], None, ALU.mult).then_inc(a6["csel"], 1)
                    for half in range(2):
                        h = g + 4 * half
                        dve.tensor_copy(GTS[:, :, half, 1:4], GT[:, :, bass.ds(3 * h, 3)]).then_inc(a6["stg"], 1)
                        dve.tensor_scalar(ALB[:, half, :], DM[:, :], SL[:, bass.ds(h, 1)], None, ALU.mult).then_inc(a6["stg"], 1)
                        dve.tensor_scalar(CLB[:, half, :, :], DC[:, :, :], SL[:, bass.ds(h, 1)], None, ALU.mult).then_inc(a6["stg"], 1)
                    dve.wait_ge(a6["stg"], 7 * g + 7)
                if t == 3:
                    heads(g)
            phase_splits("att6", dve, dve_step, evac6)

            def m_phase(name, r):
                dve_clear_acc(nj[r])
                if name.startswith("ffo"):
                    phase_splits(name, dve, dve_step, lambda g, t: dve_m(nj[r], name, 2 * g + t // 2, t // 2, g) if t % 2 else None)
                else:
                    phase_splits(name, dve, dve_step, lambda g, t: dve_m(nj[r], name, 4 * g + t, t % 2, 2 * g + t // 2))

            m_phase("att_out", "r1")
            dve_diag(nj["r1"], D)
            dve_add_normed(nj["r1"], xs[1])
            dve_diag(nj["q1"], D)
            dve.wait_ge(xs[1], C)
            dve_parts(nj["q1"], C, lambda k: X[:, k, :], lambda k: vcol("norm_g2", 16 + k))
            phase_splits("ffi1", dve, dve_step, lambda g, t: dve_ffi("ffi1", ff[1], g, t))
            dve.wait_ge(ff[1]["hid_lo"], CF)
            m_phase("ffo1", "r2")
            dve_diag(nj["r2"], D)
            dve_add_normed(nj["r2"], xs[2])
            dve_diag(nj["q2"], D)
            dve.wait_ge(xs[2], C)
            dve.wait_ge(n_rb, nj["q2"].count)
            dve.wait_ge(p10["z"], 1)
            dve.reciprocal(PINV[:, :, :], PINV[:, :, :]).then_inc(p10["inv"], 1)

            def pool_u(k):
                dve.scalar_tensor_tensor(PUT[:, k, :], X[:, k, :], vcol("norm_g2", 32 + k), RB[:, :], ALU.mult,
                                         ALU.mult).then_inc(p10["u"], 1)

            def pool_scan(k):
                dve.wait_ge(p10["u"], k + 1)
                if k >= 2:
                    dve.wait_ge(p10["e"], k - 1)
                dve.tensor_tensor_scan(PCS[:, k % 2, 16:], ONE[:, 0:1].to_broadcast([P, S]), PUT[:, k, :], 0.0,
                                       ALU.mult, ALU.add).then_inc(p10["cs"], 1)

            def pool_mean(k):
                dve.wait_ge(p10["e"], k + 1)
                if k == 0:
                    dve.wait_ge(p10["inv"], 1)
                dve.tensor_tensor(PTM[:, k % 2, 0:16], PTM[:, k % 2, 0:16], PINV[:, k // 2, :], ALU.mult).then_inc(p10["h"], 1)
                dve.scalar_tensor_tensor(PIN[:, k, 16:], PTM[:, k % 2, 16:], 0.5 ** (k // 2 + 1), PUT[:, k, 16:],
                                         ALU.mult, ALU.subtract)
                dve.wait_ge(p10["h"], k + 1)
                dve.tensor_tensor(PIN[:, k, 0:16], PTM[:, k % 2, 0:16], PUT[:, k, 0:16], ALU.subtract).then_inc(p10["in"], 1)

            pool_u(0)
            for k in range(C):
                if k + 1 < C:
                    pool_u(k + 1)
                pool_scan(k)
                if k >= 1:
                    pool_mean(k - 1)
            pool_mean(C - 1)
            dve_clear_acc(nj["r3"])
            for o in range(C):
                dve_m(nj["r3"], "pool", o, o % 2, o // 2)
            split_lo(N0["ffi2"], 0, 0, C)
            split_lo(N0["ffi2"] + 1, 1, 1, C)
            dve_diag(nj["r3"], D)
            dve_add_normed(nj["r3"], xs[3])
            dve_diag(nj["q3"], D)
            dve.wait_ge(xs[3], C)
            dve_parts(nj["q3"], C, lambda k: X[:, k, :], lambda k: vcol("norm_g2", 48 + k))
            phase_splits("ffi2", dve, dve_step, lambda g, t: dve_ffi("ffi2", ff[2], g, t))
            dve.wait_ge(ff[2]["hid_lo"], CF)
            m_phase("ffo2", "r4")
            dve_diag(nj["r4"], D)
            dve_add_normed(nj["r4"], xs[4])


def _blocks(w):
    k, m = w.shape
    return w.reshape(k // P, P, m // P, P).transpose(2, 1, 0, 3).reshape(m // P, P, k)


def _down(w):
    return w.reshape(2, KH, P, C, P).transpose(3, 0, 2, 1, 4).reshape(2 * C, P, KH * P)


def _cols(v):
    return v.reshape(-1, P).T


def _layout(a):
    w = a["w_in"][0]
    u, v, val, gate = (_blocks(w[:, i * DA:(i + 1) * DA]) for i in range(4))
    order = [x for c in range(CA) for x in (val[c:c + 1], gate[c:c + 1])] + [v, u]
    b = _cols(a["b_in"][0])
    bu, bv, bval, bgate = (b[:, 4 * i:4 * i + 4] for i in range(4))
    b_cols = [x for c in range(CA) for x in (bval[:, c:c + 1], bgate[:, c:c + 1])] + [bv, bu]
    conv = a["b_conv_w"][0].T.reshape(CA, P, TAPS).transpose(1, 0, 2).reshape(P, CA * TAPS)
    vec = np.concatenate([
        _cols(a["c"][0]), _cols(a["ada_b"][0]), _cols(a["ada_f_b"]), _cols(a["norm1_g"][0]), _cols(a["norm2_g"][0]),
        _cols(a["norm_f_g"]), *b_cols, _cols(a["b_gn_g"][0]), _cols(a["b_gn_b"][0]), _cols(a["b_conv_b"][0]), conv,
        _cols(a["out_norm_a_g"][0]), _cols(a["out_norm_b_g"][0]), _cols(a["norm_g_2"].reshape(-1)),
        _cols(a["pool_scale_2"][0])], axis=1)
    f = _blocks(a["w_ffn_in"][0])
    gu = lambda g_, u_: np.stack([g_, u_], axis=1).reshape(2 * CF, P, D)
    t = a["attn_w_in_2"][0]
    fq, fk, fv = (t[:, 512 * i:512 * (i + 1)] for i in range(3))
    ffw, nq, rest, ng = t[:, 1536:1544], t[:, 1544:2056], t[:, 2056:2824], t[:, 2824:2848]
    pad = lambda m: np.concatenate([m, np.zeros((D, P - m.shape[1]), m.dtype)], axis=1)
    pair = lambda m: m.reshape(m.shape[0], 2, 4, DH).transpose(0, 2, 1, 3).reshape(m.shape[0], 512)
    nqb, fqb, fkb, fvb = _blocks(pair(nq)), _blocks(fq), _blocks(fk), _blocks(fv)
    att = np.concatenate([_blocks(pad(ffw)), _blocks(pad(ng)), _blocks(rest)] +
                         [x[c:c + 1] for c in range(4) for x in (fqb, fkb, fvb, nqb)])
    ow = a["attn_w_out_2"][0]
    ow = np.concatenate([ow[:512], ow[512:].reshape(2, 4, DH, D).transpose(1, 0, 2, 3).reshape(512, D)])
    pw = a["pool_w_2"][0].reshape(4, 2, P, 2, P).transpose(0, 2, 3, 1, 4).reshape(4, P, 4 * P)
    out = {
        "xT": a["x"][0].T.reshape(C, P, S).transpose(1, 0, 2), "vec": vec,
        "ada_w": np.concatenate([a["ada_w"][0], a["ada_f_w"]], axis=1).reshape(C, P, ADA_N, D).transpose(
            2, 0, 1, 3).reshape(ADA_N * C, P, D),
        "w_in": np.concatenate(order), "w_out": _blocks(a["w_out"][0]), "ffi": gu(f[:CF], f[CF:]),
        "ffo": _down(a["w_ffn_out"][0]), "ln_rows": np.stack([a["a_ln_g"][0], a["a_ln_b"][0]]),
        "ws": a["a_spatial_w"][0].transpose(2, 0, 1), "bs": a["a_spatial_b"][0], "att_w": att,
        "att_out": _blocks(ow), "bf": a["fox_b_f_2"][0].reshape(NH, 1), "pe": a["nsa_cmp_pe_2"][0].transpose(2, 0, 1),
        "w1": a["nsa_cmp_w1_2"][0].reshape(2, CMPB, DH, DH).transpose(2, 0, 1, 3),
        "w2": a["nsa_cmp_w2_2"][0].transpose(1, 0, 2), "pool_w": pw,
        "f2i": np.concatenate([gu(_blocks(a["ffn_w_gate_2"][i]), _blocks(a["ffn_w_up_2"][i])) for i in range(2)]),
        "f2o": np.concatenate([_down(a["ffn_w_down_2"][i]) for i in range(2)]),
    }
    return {k: np.ascontiguousarray(v) for k, v in out.items()}


def kernel(**inputs):
    import concourse.bacc as bacc
    from concourse.bass_utils import run_bass_kernel_spmd

    nc = bacc.Bacc("TRN2", target_bir_lowering=False, num_devices=1)
    arrays = {f"in_{k}": v for k, v in _layout({k: np.asarray(v) for k, v in inputs.items()}).items()}
    args = [nc.dram_tensor(k, v.shape, mybir.dt.from_np(v.dtype), kind="ExternalInput").ap()
            for k, v in arrays.items()]
    out = nc.dram_tensor("out_T", (P, C, S), F32, kind="ExternalOutput").ap()
    build_program(nc, *args, out)
    r = run_bass_kernel_spmd(nc, [arrays], core_ids=[0])
    got = r.results[0]["out_T"]
    return np.ascontiguousarray(got.transpose(1, 0, 2).reshape(D, S).T).reshape(1, S, D)
```
